# Optimizing a Trainium2 kernel written in Bass

```python
import jax, jax.numpy as jnp
from jax import lax
import numpy as np

D_MODEL = 1024
BATCH = 1
SEQ = 256
DEPTH = 2

HEAD_DIM = 64
MIX_HEADS = D_MODEL // HEAD_DIM
A_HEADS = MIX_HEADS // 2
B_HEADS = MIX_HEADS - A_HEADS
C_HEADS = MIX_HEADS
C_KV_HEADS = max(1, C_HEADS // 8)
A_WIDTH = A_HEADS * HEAD_DIM
B_WIDTH = B_HEADS * HEAD_DIM
C_WIDTH = C_HEADS * HEAD_DIM
C_KV_WIDTH = C_KV_HEADS * HEAD_DIM
EVEN_IN = 4 * A_WIDTH + 4 * B_WIDTH
ODD_IN = 2 * C_WIDTH + 2 * C_KV_WIDTH
DILATED_PAIRS = ((128, 1), (512, 4), (2048, 16))
MOBA_BLOCK = 256
MOBA_TOPK = 3
MOBA_QCHUNK = 32
C_WINDOW = 128
BAND_BLOCK = 128
ROPE_THETA = 10000.0
NORM_EPS = 1e-6
NEG_INF = -1e30
N_EVEN = (DEPTH + 1) // 2
N_ODD = DEPTH // 2

kernel_name = "hybrid_dilated_moba_swa_sink_trunk"

def rms_norm(x, g):
    xf = x.astype(jnp.float32)
    xf = xf * lax.rsqrt(jnp.mean(xf * xf, axis=-1, keepdims=True) + NORM_EPS)
    return xf.astype(x.dtype) * g

def rope_tables(seq):
    pos = jnp.arange(seq, dtype=jnp.float32)
    inv_freq = ROPE_THETA ** (-jnp.arange(0, HEAD_DIM, 2, dtype=jnp.float32) / HEAD_DIM)
    ang = pos[:, None] * inv_freq[None, :]
    ang = jnp.concatenate([ang, ang], axis=-1)
    return jnp.cos(ang), jnp.sin(ang)

def apply_rope(t, cos, sin):
    tf = t.astype(jnp.float32)
    t1, t2 = jnp.split(tf, 2, axis=-1)
    rot = jnp.concatenate([-t2, t1], axis=-1)
    return (tf * cos + rot * sin).astype(t.dtype)

def qk_prep(t, g, cos, sin):
    return apply_rope(rms_norm(t, g), cos, sin)

def to_heads(t, n_heads):
    b, s, _ = t.shape
    return t.reshape(b, s, n_heads, HEAD_DIM).transpose(0, 2, 1, 3)

def from_heads(t):
    b, h, s, d = t.shape
    return t.transpose(0, 2, 1, 3).reshape(b, s, h * d)

def split_cols(t, widths):
    parts, start = [], 0
    for w in widths:
        parts.append(t[..., start:start + w])
        start += w
    return parts

def banded_attention(q, k, v, max_dist, sinks=None):
    n, hk, g, seq, d = q.shape
    nq = -(-seq // BAND_BLOCK)
    lp = nq * BAND_BLOCK
    qb = jnp.pad(q, ((0, 0), (0, 0), (0, 0), (0, lp - seq), (0, 0))).reshape(n, hk, g, nq, BAND_BLOCK, d)
    kv_pad = ((0, 0), (0, 0), (BAND_BLOCK, lp - seq), (0, 0))

    def windows(t):
        tb = jnp.pad(t, kv_pad).reshape(n, hk, nq + 1, BAND_BLOCK, d)
        return jnp.concatenate([tb[:, :, :-1], tb[:, :, 1:]], axis=3)

    kw, vw = windows(k), windows(v)
    s = jnp.einsum('nhgcqd,nhckd->nhgcqk', qb, kw, preferred_element_type=jnp.float32) * (d ** -0.5)
    blk = jnp.arange(nq)[:, None, None]
    qi = jnp.arange(BAND_BLOCK)[None, :, None]
    kj = jnp.arange(2 * BAND_BLOCK)[None, None, :]
    dist = BAND_BLOCK + qi - kj
    kpos = (blk - 1) * BAND_BLOCK + kj
    mask = (dist >= 0) & (dist <= max_dist) & (kpos >= 0)
    s = jnp.where(mask, s, NEG_INF)
    m = jnp.max(s, axis=-1)
    if sinks is not None:
        sk = sinks.astype(jnp.float32)[None, :, :, None, None]
        m = jnp.maximum(m, sk)
    p = jnp.exp(s - m[..., None])
    l = jnp.sum(p, axis=-1)
    if sinks is not None:
        l = l + jnp.exp(sk - m)
    o = jnp.einsum('nhgcqk,nhckd->nhgcqd', p, vw.astype(jnp.float32)) / l[..., None]
    lse = m + jnp.log(l)
    o = o.reshape(n, hk, g, lp, d)[:, :, :, :seq]
    lse = lse.reshape(n, hk, g, lp)[:, :, :, :seq]
    return o, lse

def dilated_mixture_attention(q, k, v):
    b, h, seq, d = q.shape
    outs, lses = [], []
    for window, dil in DILATED_PAIRS:
        sub = seq // dil

        def to_sub(t):
            return t.reshape(b, h, sub, dil, d).transpose(0, 3, 1, 2, 4).reshape(b * dil, h, sub, d)

        o, lse = banded_attention(to_sub(q)[:, :, None], to_sub(k), to_sub(v), window // dil)
        outs.append(o[:, :, 0].reshape(b, dil, h, sub, d).transpose(0, 2, 3, 1, 4).reshape(b, h, seq, d))
        lses.append(lse[:, :, 0].reshape(b, dil, h, sub).transpose(0, 2, 3, 1).reshape(b, h, seq))
    w = jax.nn.softmax(jnp.stack(lses, axis=0), axis=0)
    return jnp.sum(w[..., None] * jnp.stack(outs, axis=0), axis=0)

def moba_attention(q, k, v):
    b, h, seq, d = q.shape
    nb = -(-seq // MOBA_BLOCK)
    sp = nb * MOBA_BLOCK
    pad = ((0, 0), (0, 0), (0, sp - seq), (0, 0))
    qp, kp, vp = jnp.pad(q, pad), jnp.pad(k, pad), jnp.pad(v, pad)
    kb = kp.reshape(b, h, nb, MOBA_BLOCK, d)
    vb = vp.reshape(b, h, nb, MOBA_BLOCK, d)
    scale = d ** -0.5
    own_blk = jnp.arange(sp) // MOBA_BLOCK
    n_sel = min(MOBA_TOPK, nb - 1)
    nc = sp // MOBA_QCHUNK

    def to_chunks(t):
        return jnp.moveaxis(t.reshape(b, h, nc, MOBA_QCHUNK, t.shape[-1]), 2, 0)

    xs = [jnp.arange(nc), to_chunks(qp)]
    if n_sel > 0:
        kmean = jnp.mean(kb.astype(jnp.float32), axis=3)
        gate = jnp.einsum('bhsd,bhnd->bhsn', qp.astype(jnp.float32), kmean)
        past = jnp.arange(nb)[None, :] < own_blk[:, None]
        gate = jnp.where(past, gate, NEG_INF)
        _, sel = lax.top_k(gate, n_sel)
        sel_valid = sel < own_blk[:, None]
        xs += [to_chunks(sel), to_chunks(sel_valid)]
    bi = jnp.arange(b)[:, None, None]
    hi = jnp.arange(h)[None, :, None]
    offs = jnp.arange(MOBA_BLOCK)

    def one_chunk(args):
        c, qc = args[0], args[1]
        qpos = c * MOBA_QCHUNK + jnp.arange(MOBA_QCHUNK)
        blk = (c * MOBA_QCHUNK) // MOBA_BLOCK
        k_own = lax.dynamic_slice_in_dim(kp, blk * MOBA_BLOCK, MOBA_BLOCK, axis=2)
        v_own = lax.dynamic_slice_in_dim(vp, blk * MOBA_BLOCK, MOBA_BLOCK, axis=2)
        s_own = jnp.einsum('bhqd,bhkd->bhqk', qc, k_own, preferred_element_type=jnp.float32) * scale
        causal = (blk * MOBA_BLOCK + offs)[None, :] <= qpos[:, None]
        s_own = jnp.where(causal, s_own, NEG_INF)
        if n_sel == 0:
            p = jax.nn.softmax(s_own, axis=-1)
            return jnp.einsum('bhqk,bhkd->bhqd', p, v_own.astype(jnp.float32))
        selc, validc = args[2], args[3]
        flat = selc.reshape(b, h, MOBA_QCHUNK * n_sel)
        k_sel = kb[bi, hi, flat].reshape(b, h, MOBA_QCHUNK, n_sel * MOBA_BLOCK, d)
        v_sel = vb[bi, hi, flat].reshape(b, h, MOBA_QCHUNK, n_sel * MOBA_BLOCK, d)
        s_sel = jnp.einsum('bhqd,bhqkd->bhqk', qc, k_sel, preferred_element_type=jnp.float32) * scale
        s_sel = jnp.where(jnp.repeat(validc, MOBA_BLOCK, axis=-1), s_sel, NEG_INF)
        p = jax.nn.softmax(jnp.concatenate([s_sel, s_own], axis=-1), axis=-1)
        nsk = n_sel * MOBA_BLOCK
        return (jnp.einsum('bhqk,bhqkd->bhqd', p[..., :nsk], v_sel.astype(jnp.float32))
                + jnp.einsum('bhqk,bhkd->bhqd', p[..., nsk:], v_own.astype(jnp.float32)))

    out = lax.map(one_chunk, tuple(xs))
    return jnp.moveaxis(out, 0, 2).reshape(b, h, sp, d)[:, :, :seq]

def sliding_window_sink_attention(q, k, v, sinks):
    b, hq, seq, d = q.shape
    g = hq // C_KV_HEADS
    o, _ = banded_attention(q.reshape(b, C_KV_HEADS, g, seq, d), k, v, C_WINDOW - 1,
                            sinks.reshape(C_KV_HEADS, g))
    return o.reshape(b, hq, seq, d)

def even_layer(x, g_norm, w_in, w_out, qn_a, kn_a, qn_b, kn_b, cos, sin):
    h = rms_norm(x, g_norm)
    proj = h @ w_in
    qa, ka, va, za, qb, kb, vb, zb = split_cols(proj, [A_WIDTH] * 4 + [B_WIDTH] * 4)
    qa = qk_prep(to_heads(qa, A_HEADS), qn_a, cos, sin)
    ka = qk_prep(to_heads(ka, A_HEADS), kn_a, cos, sin)
    qb = qk_prep(to_heads(qb, B_HEADS), qn_b, cos, sin)
    kb = qk_prep(to_heads(kb, B_HEADS), kn_b, cos, sin)
    oa = dilated_mixture_attention(qa, ka, to_heads(va, A_HEADS))
    ob = moba_attention(qb, kb, to_heads(vb, B_HEADS))
    y = from_heads(jnp.concatenate([oa, ob], axis=1)).astype(x.dtype)
    z = jnp.concatenate([za, zb], axis=-1)
    return x + (y * jax.nn.silu(z)) @ w_out

def odd_layer(x, g_norm, w_in, w_out, qn_c, kn_c, sinks, cos, sin):
    h = rms_norm(x, g_norm)
    proj = h @ w_in
    qc, kc, vc, zc = split_cols(proj, [C_WIDTH, C_KV_WIDTH, C_KV_WIDTH, C_WIDTH])
    qc = qk_prep(to_heads(qc, C_HEADS), qn_c, cos, sin)
    kc = qk_prep(to_heads(kc, C_KV_HEADS), kn_c, cos, sin)
    oc = sliding_window_sink_attention(qc, kc, to_heads(vc, C_KV_HEADS), sinks)
    y = from_heads(oc).astype(x.dtype)
    return x + (y * jax.nn.silu(zc)) @ w_out

def setup_inputs(seed: int = 0) -> dict:
    key = jax.random.key(seed)
    ks = jax.random.split(key, 16)

    def normal(k, shape, scale):
        return jax.random.normal(k, shape, jnp.float32) * scale

    def gain(k, shape):
        return 1.0 + 0.05 * jax.random.normal(k, shape, jnp.float32)

    return {
        'x': normal(ks[0], (BATCH, SEQ, D_MODEL), 1.0),
        'norm_even': gain(ks[1], (N_EVEN, D_MODEL)),
        'w_in_even': normal(ks[2], (N_EVEN, D_MODEL, EVEN_IN), D_MODEL ** -0.5),
        'w_out_even': normal(ks[3], (N_EVEN, A_WIDTH + B_WIDTH, D_MODEL), (A_WIDTH + B_WIDTH) ** -0.5),
        'qnorm_a': gain(ks[4], (N_EVEN, HEAD_DIM)),
        'knorm_a': gain(ks[5], (N_EVEN, HEAD_DIM)),
        'qnorm_b': gain(ks[6], (N_EVEN, HEAD_DIM)),
        'knorm_b': gain(ks[7], (N_EVEN, HEAD_DIM)),
        'norm_odd': gain(ks[8], (N_ODD, D_MODEL)),
        'w_in_odd': normal(ks[9], (N_ODD, D_MODEL, ODD_IN), D_MODEL ** -0.5),
        'w_out_odd': normal(ks[10], (N_ODD, C_WIDTH, D_MODEL), C_WIDTH ** -0.5),
        'qnorm_c': gain(ks[11], (N_ODD, HEAD_DIM)),
        'knorm_c': gain(ks[12], (N_ODD, HEAD_DIM)),
        'sinks_c': normal(ks[13], (N_ODD, C_HEADS), 1.0),
    }

def reference(x, norm_even, w_in_even, w_out_even, qnorm_a, knorm_a, qnorm_b, knorm_b,
              norm_odd, w_in_odd, w_out_odd, qnorm_c, knorm_c, sinks_c):
    cos, sin = rope_tables(x.shape[1])
    for layer in range(DEPTH):
        i = layer // 2
        if layer % 2 == 0:
            x = even_layer(x, norm_even[i], w_in_even[i], w_out_even[i],
                           qnorm_a[i], knorm_a[i], qnorm_b[i], knorm_b[i], cos, sin)
        else:
            x = odd_layer(x, norm_odd[i], w_in_odd[i], w_out_odd[i],
                          qnorm_c[i], knorm_c[i], sinks_c[i], cos, sin)
    return x


_drawn_inputs = setup_inputs


def setup_inputs(seed=0):
    import zlib

    import numpy as np

    out = dict(_drawn_inputs(seed))
    spreads = {}
    factors = {'norm_even': 4.13,
     'qnorm_a': 8.0,
     'knorm_a': 8.0,
     'qnorm_b': 8.0,
     'knorm_b': 8.0,
     'norm_odd': 5.367,
     'qnorm_c': 8.0,
     'knorm_c': 8.0,
     'sinks_c': 20.188}
    for name, (base, spread) in spreads.items():
        noise = np.random.default_rng([zlib.crc32(name.encode()), seed]).standard_normal(out[name].shape)
        drawn = base * np.exp(spread * noise) if base else spread * noise
        out[name] = __import__('jax').numpy.asarray(drawn.astype(out[name].dtype))
    for name, factor in factors.items():
        out[name] = (out[name] * factor).astype(out[name].dtype)
    return out
```

```python
from contextlib import ExitStack

import numpy as np

import concourse.bass as bass
from concourse import mybir

F32 = mybir.dt.float32
F32R = mybir.dt.float32r
ALU = mybir.AluOpType
ACT = mybir.ActivationFunctionType
AX_X = mybir.AxisListType.X

P = 128
S = 256
T = S // P
D = 1024
K = D // P
HD = 64
HA = 8
HC = 16
NCOL = 512
CH = NCOL // HD
VW = HD + 1
EPS = 1e-6
NEG = -1e30
BIG = 3e38
ROPE_THETA = 10000.0
WINDOW = 128

CHUNKS = ([(n, NCOL) for n in ("qA", "kA", "vA", "qB", "kB", "vB", "zA", "zB", "o0", "o1")]
          + [("kvC", 256)] + [(n, NCOL) for n in ("qC0", "qC1", "zC0", "zC1", "p0", "p1")])
CHUNK = {n: i for i, (n, _) in enumerate(CHUNKS)}
PIECE = 1024
KPP = [PIECE // w for _, w in CHUNKS]
PIECES = [K // kpp for kpp in KPP]
FIRST_PIECE = [sum(PIECES[:i]) for i in range(len(CHUNKS))]
N_PIECES = sum(PIECES)
PER_DMA = 2
N_DMAS = N_PIECES // PER_DMA
RAW = 3
RING = 9

UNITS = [(c, t) for c in ("qA", "kA", "vA", "qB", "kB", "vB", "zA", "zB") for t in range(T)]
UNITS += [("o0", 0), ("o1", 0), ("o0", 1), ("o1", 1)]
UNITS += [("kvC", 0), ("qC0", 0), ("kvC", 1), ("qC0", 1), ("qC1", 0), ("qC1", 1)]
UNITS += [("zC0", 0), ("zC0", 1), ("zC1", 0), ("zC1", 1)]
UNITS += [("p0", 0), ("p1", 0), ("p0", 1), ("p1", 1)]
UNIT = {u: i for i, u in enumerate(UNITS)}


def is_out(u):
    return UNITS[u][0][0] in "op"


QK = [u for u, (c, _) in enumerate(UNITS) if c[0] in "qk"]
ZU = [u for u, (c, _) in enumerate(UNITS) if c[0] == "z"]
VU = [u for u, (c, _) in enumerate(UNITS) if c[0] == "v"]
STAGED = [u for u in range(len(UNITS)) if u in QK or u in ZU]
PROJ = [u for u in range(len(UNITS)) if not is_out(u)]
OUTS = [u for u in range(len(UNITS)) if is_out(u)]

PARTS = {"q": 2, "k": 2, "v": 2, "z": 2, "o": 2, "kvC": 1, "qC0": 2, "qC1": 3, "zC0": 3, "zC1": 3, "p": 2}
GAP_B, GAP_C = 2, 3
SLOTS = []
for _u, (_c, _t) in enumerate(UNITS):
    if (_c, _t) == ("o0", 0):
        SLOTS += [(None, 0, 1)] * GAP_B
    if (_c, _t) == ("p0", 0):
        SLOTS += [(None, 0, 1)] * GAP_C
    _n = PARTS[_c] if _c in PARTS else PARTS[_c[0]]
    SLOTS += [(_u, i, _n) for i in range(_n)]
N_SLOTS = len(SLOTS)
BEGIN = {u: min(n for n, s in enumerate(SLOTS) if s[0] == u) for u in range(len(UNITS))}
END = {u: max(n for n, s in enumerate(SLOTS) if s[0] == u) for u in range(len(UNITS))}

STEPS = [("A", h) for h in range(HA)] + [("B", h) for h in range(HA)] + [("C", h) for h in range(HC)]
N_STEPS = len(STEPS)
A_SLOTS = [END[UNIT["kA", 1]] + d for d in (4, 5, 7, 8, 10, 11, 13, 14)]
B_SLOTS = [END[UNIT["kB", 1]] + 4 + d for d in range(HA)]
C_SLOTS = ([END[UNIT["qC0", 1]] + 4 + d for d in range(HA)]
           + [END[UNIT["qC1", 1]] + 6 + d for d in range(HA)])
STEP_AT = {n: s for s, n in enumerate(A_SLOTS + B_SLOTS + C_SLOTS)}
assert len(STEP_AT) == N_STEPS

TURN_AT = {}
for _i, _u in enumerate(QK):
    TURN_AT.setdefault(END[_u] + 3, []).append(_i)

BATCHES = [(0, 0, 0), (0, 0, 1), (0, 1, 0), (0, 1, 1),
           (1, 0, 0), (1, 0, 1), (1, 1, 0), (1, 1, 1),
           (2, 0, 0), (2, 0, 1), (2, 1, 0), (2, 1, 1),
           (3, 0, 0), (3, 0, 1), (3, 1, 0), (3, 1, 1)]
BATCH = {b: i for i, b in enumerate(BATCHES)}
BATCH_AT = {0: [0, 1, 2, 3],
            BEGIN[UNIT["o0", 0]]: [4, 5, 6, 7],
            BEGIN[UNIT["kvC", 0]]: [8, 9],
            BEGIN[UNIT["kvC", 1]]: [10, 11],
            BEGIN[UNIT["p0", 0]]: [12, 13, 14, 15]}

JOBS = []
for _n in range(N_SLOTS):
    JOBS += [("turn", i) for i in TURN_AT.get(_n, [])]
    JOBS += [("probs", STEP_AT[_n - 1])] if _n - 1 in STEP_AT else []
    JOBS += [("batch", b) for b in BATCH_AT.get(_n, [])]
JOB = {j: i for i, j in enumerate(JOBS)}


def last_use(piece):
    c = max(i for i in range(len(CHUNKS)) if FIRST_PIECE[i] <= piece)
    return max(UNIT[CHUNKS[c][0], t] for t in range(T))


def split_slots():
    out = {-1: list(range(5))}
    p = 5
    for n in range(N_SLOTS):
        out[n] = []
        while p < N_PIECES and (p < RING or END[last_use(p - RING)] < n):
            c = max(i for i in range(len(CHUNKS)) if FIRST_PIECE[i] <= p)
            use = min(BEGIN[UNIT[CHUNKS[c][0], t]] for t in range(T))
            if len(out[n]) >= (1 if use > n + 2 and SLOTS[n][2] > 1 else 2):
                break
            out[n].append(p)
            p += 1
    assert p == N_PIECES
    return out


SPLIT_AT = split_slots()


def bass_hybrid_dilated_moba_swa_sink_trunk(nc, x_d, w_d, gains_d, heads_d, cos_d, sin_d, masks_d, sinks_d, out_d):
    with ExitStack() as ctx:
        def sb(name, shape, dt=F32):
            return ctx.enter_context(nc.sbuf_tensor(name, shape, dt))

        def pb(name):
            return ctx.enter_context(nc.psum_tensor(name, [P, 512], F32))

        def sem(name):
            return ctx.enter_context(nc.semaphore(name))

        x_sb = sb("x_sb", [P, T, D])
        gains = sb("gains", [P, 2, D])
        head_g = sb("head_g", [P, 2, 6, HD])
        cos_sb = sb("cos_sb", [P, T, HD])
        sin_sb = sb("sin_sb", [P, T, HD])
        rope_c = sb("rope_c", [P, T, 6, HD])
        rope_s = sb("rope_s", [P, T, 6, HD])
        masks = sb("masks", [P, 3, 2 * P])
        count = sb("count", [P, 2 * P])
        sinks = sb("sinks", [P, HC])
        neg_sinks = sb("neg_sinks", [P, HC])
        ident = sb("ident", [P, P])
        minus_half = sb("minus_half", [P, CH])
        raw = sb("raw", [P, RAW, PER_DMA, PIECE])
        w_hi = sb("w_hi", [P, RING, PIECE], F32R)
        w_lo = sb("w_lo", [P, RING, PIECE], F32R)
        a_hi = sb("a_hi", [P, K, S], F32R)
        a_lo = sb("a_lo", [P, K, S], F32R)
        act_src = sb("act_src", [P, T, D])
        stage = sb("stage", [P, 2, NCOL])
        stage2 = sb("stage2", [P, 2, NCOL])
        rot_a = sb("rot_a", [P, NCOL])
        rot_b = sb("rot_b", [P, NCOL])
        rot = sb("rot", [P, 2, NCOL])
        msq = sb("msq", [P, 2, CH])
        r_tmp = sb("r_tmp", [P, 2, CH])
        r_key = sb("r_key", [P, 2, CH])
        r_qry = sb("r_qry", [P, 8, CH])
        qk_t = sb("qk_t", [P, 16, S])
        kc_t = sb("kc_t", [P, S])
        va = sb("va", [P, T, HA, VW])
        vb = sb("vb", [P, T, HA, VW])
        vc = sb("vc", [P, T, 2, VW])
        probs = sb("probs", [P, 2, 3 * P])
        probs_t = sb("probs_t", [P, 2, 3 * P])
        neg_m = sb("neg_m", [P, HC, T])
        y = sb("y", [P, T, HC, VW])
        inv_l = sb("inv_l", [P, T, HC])
        sink_e = sb("sink_e", [P, HC, T])
        ssq = sb("ssq", [P, 4, 2])
        ms = sb("ms", [P, 4])
        rstd = sb("rstd", [P, 4])

        acc = [pb(f"acc{i}") for i in range(2)]
        sc = [pb(f"sc{i}") for i in range(2)]
        tp = [pb(f"tp{i}") for i in range(2)]
        ob = [pb(f"ob{i}") for i in range(2)]

        x_in = [sem(f"x_in{t}") for t in range(T)]
        gains_in = sem("gains_in")
        tables_in = sem("tables_in")
        masks_in = sem("masks_in")
        raw_in = [sem(f"raw_in{i}") for i in range(RAW)]
        hi_done = sem("hi_done")
        lo_done = sem("lo_done")
        const_done = sem("const_done")
        gp_chain = sem("gp_chain")
        dve_chain = sem("dve_chain")
        sumsq_done = sem("sumsq_done")
        rstd_done = sem("rstd_done")
        normed = sem("normed")
        turned = sem("turned")
        a_hi_done = sem("a_hi_done")
        a_lo_done = sem("a_lo_done")
        proj_done = sem("proj_done")
        out_added = sem("out_added")
        staged = sem("staged")
        msq_done = sem("msq_done")
        qk_rstd = sem("qk_rstd")
        rotated = sem("rotated")
        silu_done = sem("silu_done")
        qk_turned = sem("qk_turned")
        qk_ready = sem("qk_ready")
        v_ready = sem("v_ready")
        scores_done = sem("scores_done")
        masked = sem("masked")
        exp_done = sem("exp_done")
        weighted = sem("weighted")
        probs_turned = sem("probs_turned")
        probs_copied = sem("probs_copied")
        head_done = sem("head_done")
        head_copied = sem("head_copied")
        sinks_added = sem("sinks_added")
        sinks_exp = sem("sinks_exp")
        gated = sem("gated")
        stored = sem("stored")

        block = ctx.enter_context(nc.Block())

        def parts_of(name):
            c = CHUNK[name]
            return CHUNKS[c][1], KPP[c], FIRST_PIECE[c]

        def bank_free(eng, j):
            if j >= 2:
                kind, i = JOBS[j - 2]
                if kind == "turn":
                    eng.wait_ge(qk_ready, i + 1)
                elif kind == "probs":
                    eng.wait_ge(probs_copied, i + 1)
                else:
                    eng.wait_ge(a_lo_done, i + 1)

        def query_scale(mixer, h, t):
            col = {"A": 0, "B": 2, "C": 4 + 2 * (h // CH)}[mixer] + t
            return r_qry[:, col, h % CH:h % CH + 1]

        def q_of(mixer, h):
            side = HD * (h % 2)
            return qk_t[side:side + HD, {"A": 0, "B": 8, "C": 0}[mixer] + h // 2, :]

        def k_of(mixer, h):
            side = HD * (h % 2)
            if mixer == "C":
                return kc_t[side:side + HD, :]
            return qk_t[side:side + HD, {"A": 4, "B": 12}[mixer] + h // 2, :]

        def v_of(mixer, h, t):
            if mixer == "C":
                return vc[:, t, h % 2, :]
            return (va if mixer == "A" else vb)[:, t, h, :]

        SCORES_NEED = {"A": QK.index(UNIT["kA", 1]), "B": QK.index(UNIT["kB", 1]),
                       "C0": QK.index(UNIT["qC0", 1]), "C1": QK.index(UNIT["qC1", 1])}

        @block.sync
        def _(sp):
            def load(d):
                if d >= RAW:
                    sp.wait_ge(lo_done, PER_DMA * (d - RAW + 1))
                    sp.wait_ge(hi_done, PER_DMA * (d - RAW + 1))
                sp.dma_start(raw[:, d % RAW, :, :].rearrange("p a n -> p (a n)"),
                             w_d[d, :, :]).then_inc(raw_in[d % RAW], 16)

            for t in range(T):
                sp.dma_start(x_sb[:, t, :], x_d[t * P:(t + 1) * P, :]).then_inc(x_in[t], 16)
            for d in range(N_DMAS):
                load(d)
            for i, u in enumerate(OUTS[4:]):
                name, t = UNITS[u]
                c = int(name[1]) * NCOL
                sp.wait_ge(out_added, 4 + i + 1)
                sp.dma_start(out_d[t * P:(t + 1) * P, c:c + NCOL], x_sb[:, t, c:c + NCOL]).then_inc(stored, 16)
            sp.wait_ge(stored, 16 * 4)

        @block.gpsimd
        def _(pool):
            steps = [0]

            def chain(ins):
                steps[0] += 1
                ins.then_inc(gp_chain, 1)
                pool.wait_ge(gp_chain, steps[0])

            chain(nc.gpsimd.memset(ident[:], 0.0))
            nc.gpsimd.affine_select(out=ident[:], in_=ident[:], compare_op=ALU.not_equal, fill=1.0, base=0,
                                    pattern=[[-1, P]], channel_multiplier=1).then_inc(const_done, 1)
            chain(nc.gpsimd.memset(minus_half[:], -0.5))
            for v in (va, vb, vc):
                nc.gpsimd.memset(v[:, :, :, HD:VW], 2.0).then_inc(const_done, 1)

            def row_norm(i):
                pool.wait_ge(sumsq_done, 2 * (i + 1))
                chain(nc.gpsimd.tensor_tensor(ms[:, i:i + 1], ssq[:, i, 0:1], ssq[:, i, 1:2], ALU.add))
                chain(nc.gpsimd.tensor_scalar(ms[:, i:i + 1], ms[:, i:i + 1], 1.0 / D, EPS, ALU.mult, ALU.add))
                nc.gpsimd.tensor_tensor(rstd[:, i:i + 1], ms[:, i:i + 1], minus_half[:, 0:1],
                                        ALU.pow).then_inc(rstd_done, 1)

            def head_norm(i):
                u = QK[i]
                name, t = UNITS[u]
                n = 2 if name == "kvC" else CH
                pool.wait_ge(msq_done, i + 1)
                if i >= 2:
                    pool.wait_ge(rotated, i - 1)
                    pool.wait_ge(qk_rstd, i - 1)
                chain(nc.gpsimd.tensor_scalar(r_tmp[:, i % 2, 0:n], msq[:, i % 2, 0:n], 1.0 / HD, EPS,
                                              ALU.mult, ALU.add))
                if name[0] == "k":
                    nc.gpsimd.tensor_tensor(r_key[:, i % 2, 0:n], r_tmp[:, i % 2, 0:n], minus_half[:, 0:n],
                                            ALU.pow).then_inc(qk_rstd, 1)
                else:
                    col = {"qA": 0, "qB": 2, "qC0": 4, "qC1": 6}[name] + t
                    chain(nc.gpsimd.tensor_tensor(r_qry[:, col, :], r_tmp[:, i % 2, :], minus_half[:], ALU.pow))
                    nc.gpsimd.tensor_scalar(r_qry[:, col, :], r_qry[:, col, :], -float(HD) ** -0.5, None,
                                            ALU.mult).then_inc(qk_rstd, 1)

            row_norm(0)
            row_norm(1)
            pool.wait_ge(tables_in, 48)
            for t in range(T):
                for dst, src, g in ((rope_c, cos_sb, 0), (rope_s, sin_sb, 1)):
                    nc.gpsimd.tensor_tensor(dst[:, t, :, :], head_g[:, g, :, :],
                                            src[:, t:t + 1, :].to_broadcast([P, 6, HD]),
                                            ALU.mult).then_inc(const_done, 1)
            qk_end = {}
            for i, u in enumerate(QK):
                qk_end.setdefault(END[u] + 1, []).append(i)
            for n in range(N_SLOTS):
                for i in qk_end.get(n, []):
                    head_norm(i)
                if n in STEP_AT and STEPS[STEP_AT[n]][0] == "A":
                    s = STEP_AT[n]
                    pool.wait_ge(exp_done, s + 1)
                    pool.wait_ge(masks_in, 48)
                    nc.gpsimd.tensor_tensor(probs[:, s % 2, 0:P], probs[:, s % 2, 0:P], count[:, P:2 * P], ALU.mult)
                    nc.gpsimd.tensor_tensor(probs[:, s % 2, P:3 * P], probs[:, s % 2, P:3 * P], count[:],
                                            ALU.mult).then_inc(weighted, 1)
                for t in range(T):
                    if n == END[UNIT["o1", t]] + 1:
                        row_norm(2 + t)

        @block.scalar
        def _(act):
            act.dma_start(gains[:].rearrange("p a n -> p (a n)"), gains_d.to_broadcast([P, 2 * D])).then_inc(gains_in, 16)
            act.dma_start(head_g[:].rearrange("p a b n -> p (a b n)"),
                          heads_d.to_broadcast([P, 12 * HD])).then_inc(tables_in, 16)
            act.dma_start(cos_sb[:], cos_d.rearrange("(t p) n -> p t n", p=P)).then_inc(tables_in, 16)
            act.dma_start(sin_sb[:], sin_d.rearrange("(t p) n -> p t n", p=P)).then_inc(tables_in, 16)
            act.dma_start(masks[:], masks_d[:, 0:3, :]).then_inc(masks_in, 16)
            act.dma_start(count[:], masks_d[:, 3, :]).then_inc(masks_in, 16)
            act.dma_start(sinks[:], sinks_d.to_broadcast([P, HC])).then_inc(masks_in, 16)

            def sum_squares(i, half):
                t = i % 2
                if half == 0 and i < 2:
                    act.wait_ge(x_in[t], 16)
                n = 2 * i + half
                if n >= 1:
                    act.wait_ge(sumsq_done, n)
                if i >= 2:
                    act.wait_ge(head_copied, HC)
                nc.scalar.activation(ob[0][:], x_sb[:, t, half * NCOL:(half + 1) * NCOL], ACT.Square,
                                     accum_out=ssq[:, i, half:half + 1]).then_inc(sumsq_done, 1)

            def split_hi(p):
                d = p // PER_DMA
                act.wait_ge(raw_in[d % RAW], 16 * (d // RAW + 1))
                if p >= RING:
                    act.wait_ge(proj_done, last_use(p - RING) + 1)
                nc.scalar.activation(w_hi[:, p % RING, :], raw[:, d % RAW, p % PER_DMA, :],
                                     ACT.Copy).then_inc(hi_done, 1)

            def batch_hi(b):
                phase, t, half = BATCHES[b]
                act.wait_ge(turned, b + 1)
                if phase > 0:
                    before = {1: UNIT["zB", t], 2: UNIT["o1", t], 3: UNIT["zC1", t]}[phase]
                    act.wait_ge(proj_done, before + 1)
                nc.scalar.activation(a_hi[:, 4 * half:4 * half + 4, t * P:(t + 1) * P],
                                     tp[JOB["batch", b] % 2][:].rearrange("p (k n) -> p k n", k=4),
                                     ACT.Copy).then_inc(a_hi_done, 1)

            def read_unit(u):
                name, t = UNITS[u]
                act.wait_ge(proj_done, u + 1)
                bank = acc[u % 2]
                if u in STAGED:
                    e = STAGED.index(u)
                    if e >= 2:
                        former = STAGED[e - 2]
                        if former in QK:
                            act.wait_ge(rotated, QK.index(former) + 1)
                        else:
                            act.wait_ge(silu_done, ZU.index(former) + 1)
                    width = 2 * HD if name == "kvC" else NCOL
                    nc.scalar.activation(stage[:, e % 2, 0:width], bank[:, 0:width], ACT.Copy)
                    if name == "kvC":
                        nc.scalar.activation(vc[:, t, :, 0:HD],
                                             bank[:, width:2 * width].rearrange("p (h d) -> p h d", h=2),
                                             ACT.Copy).then_inc(v_ready, 1)
                    fn, scale = (ACT.Tanh, 0.5) if name[0] == "z" else (ACT.Square, 1.0)
                    nc.scalar.activation(stage2[:, e % 2, 0:width], bank[:, 0:width], fn,
                                         scale=scale).then_inc(staged, 1)
                else:
                    v = va if name == "vA" else vb
                    nc.scalar.activation(v[:, t, :, 0:HD], bank[:].rearrange("p (h d) -> p h d", h=HA),
                                         ACT.Copy).then_inc(v_ready, 1)

            def copy_turned(i):
                name, t = UNITS[QK[i]]
                act.wait_ge(qk_turned, i + 1)
                cols = slice(t * P, (t + 1) * P)
                bank = tp[JOB["turn", i] % 2]
                if name == "kvC":
                    nc.scalar.activation(kc_t[:, cols], bank[:, 0:P], ACT.Copy).then_inc(qk_ready, 1)
                else:
                    at = {"qA": 0, "kA": 4, "qB": 8, "kB": 12, "qC0": 0, "qC1": 4}[name]
                    if name[1] == "C":
                        act.wait_ge(scores_done, HA)
                    nc.scalar.activation(qk_t[:, at:at + 4, cols], bank[:].rearrange("p (k n) -> p k n", k=4),
                                         ACT.Copy).then_inc(qk_ready, 1)

            def softmax_exp(s):
                act.wait_ge(masked, s + 1)
                c = s if s < HC else s - HC
                for t, cols in ((0, slice(0, P)), (1, slice(P, 3 * P))):
                    last = nc.scalar.activation(probs[:, s % 2, cols], probs[:, s % 2, cols], ACT.Exp,
                                                bias=neg_m[:, c, t:t + 1], scale=-1.0)
                last.then_inc(exp_done, 1)

            def copy_probs(s):
                act.wait_ge(probs_turned, s + 1)
                if s >= 2:
                    act.wait_ge(head_done, s - 1)
                nc.scalar.activation(probs_t[:, s % 2, :], tp[JOB["probs", s] % 2][:, 0:3 * P],
                                     ACT.Copy).then_inc(probs_copied, 1)

            for t in range(T):
                sum_squares(t, 0)
                sum_squares(t, 1)
            for p in SPLIT_AT[-1]:
                split_hi(p)
            for n in range(N_SLOTS):
                for i in TURN_AT.get(n, []):
                    copy_turned(i)
                if n - 1 in STEP_AT:
                    copy_probs(STEP_AT[n - 1])
                for b in BATCH_AT.get(n, []):
                    batch_hi(b)
                for u in range(len(UNITS)):
                    if n == END[u] + 1 and not is_out(u):
                        read_unit(u)
                if n in STEP_AT:
                    softmax_exp(STEP_AT[n])
                for t in range(T):
                    for half in range(2):
                        if n == END[UNIT[f"o{half}", t]] + 1:
                            act.wait_ge(out_added, 2 * t + half + 1)
                            sum_squares(2 + t, half)
                if n - 1 in STEP_AT and STEP_AT[n - 1] in (HC + CH - 1, N_STEPS - 1):
                    g = int(STEP_AT[n - 1] == N_STEPS - 1)
                    act.wait_ge(sinks_added, g + 1)
                    nc.scalar.activation(sink_e[:, g * CH:(g + 1) * CH, :], sink_e[:, g * CH:(g + 1) * CH, :],
                                         ACT.Exp).then_inc(sinks_exp, 1)
                for p in SPLIT_AT[n]:
                    split_hi(p)

        @block.tensor
        def _(pe):
            def project(n):
                u, part, parts = SLOTS[n]
                if u is None:
                    return
                name, t = UNITS[u]
                width, kpp, first = parts_of(name)
                bank = acc[u % 2][:, 0:width]
                if part == 0:
                    if u >= 2:
                        if is_out(u - 2):
                            pe.wait_ge(out_added, OUTS.index(u - 2) + 1)
                        elif u - 2 in STAGED:
                            pe.wait_ge(staged, STAGED.index(u - 2) + 1)
                        else:
                            pe.wait_ge(v_ready, VU.index(u - 2) + 1)
                    phase = 0 if u < UNIT["o0", 0] else 1 if u < UNIT["kvC", 0] else 2 if u < UNIT["p0", 0] else 3
                    pe.wait_ge(a_lo_done, BATCH[phase, t, 1] + 1)
                for k in range(K * part // parts, K * (part + 1) // parts):
                    p = first + k // kpp
                    if k % kpp == 0 or k == K * part // parts:
                        pe.wait_ge(lo_done, p + 1)
                    cols = slice((k % kpp) * width, (k % kpp + 1) * width)
                    hi, lo = w_hi[:, p % RING, cols], w_lo[:, p % RING, cols]
                    ah, al = a_hi[:, k, t * P:(t + 1) * P], a_lo[:, k, t * P:(t + 1) * P]
                    nc.tensor.matmul(bank, ah, hi, start=(k == 0), stop=False)
                    nc.tensor.matmul(bank, ah, lo, start=False, stop=False)
                    last = nc.tensor.matmul(bank, al, hi, start=False, stop=(k == K - 1))
                if part == parts - 1:
                    last.then_inc(proj_done, 1)

            def scores(s):
                mixer, h = STEPS[s]
                need = mixer if mixer != "C" else f"C{h // CH}"
                pe.wait_ge(qk_ready, SCORES_NEED[need] + 1)
                if s >= 2:
                    pe.wait_ge(masked, s - 1)
                q, k = q_of(mixer, h), k_of(mixer, h)
                nc.tensor.matmul(sc[s % 2][:, 0:P], q[:, 0:P], k[:, 0:P], start=True, stop=True)
                nc.tensor.matmul(sc[s % 2][:, P:3 * P], q[:, P:2 * P], k[:, 0:2 * P],
                                 start=True, stop=True).then_inc(scores_done, 1)

            def turn_probs(s):
                if STEPS[s][0] == "A":
                    pe.wait_ge(weighted, s + 1)
                else:
                    pe.wait_ge(exp_done, s + 1)
                bank_free(pe, JOB["probs", s])
                for i in range(3):
                    last = nc.tensor.transpose(tp[JOB["probs", s] % 2][:, i * P:(i + 1) * P],
                                               probs[:, s % 2, i * P:(i + 1) * P], ident[:])
                last.then_inc(probs_turned, 1)

            def values(s):
                mixer, h = STEPS[s]
                pe.wait_ge(probs_copied, s + 1)
                pe.wait_ge(v_ready, {"A": 2, "B": 4, "C": 6}[mixer])
                if s >= 2:
                    pe.wait_ge(head_copied, s - 1)
                if s in (0, HC):
                    pe.wait_ge(sumsq_done, 4 if s == 0 else 8)
                pt, o = probs_t[:, s % 2, :], ob[s % 2]
                nc.tensor.matmul(o[:, 0:VW], pt[:, 0:P], v_of(mixer, h, 0), start=True, stop=True)
                nc.tensor.matmul(o[:, VW:2 * VW], pt[:, P:2 * P], v_of(mixer, h, 0), start=True, stop=False)
                nc.tensor.matmul(o[:, VW:2 * VW], pt[:, 2 * P:3 * P], v_of(mixer, h, 1),
                                 start=False, stop=True).then_inc(head_done, 1)

            def turn_qk(i):
                pe.wait_ge(rotated, i + 1)
                bank_free(pe, JOB["turn", i])
                for j in range(1 if UNITS[QK[i]][0] == "kvC" else 4):
                    last = nc.tensor.transpose(tp[JOB["turn", i] % 2][:, j * P:(j + 1) * P],
                                               rot[:, i % 2, j * P:(j + 1) * P], ident[:])
                last.then_inc(qk_turned, 1)

            def turn_batch(b):
                phase, t, half = BATCHES[b]
                if phase in (0, 2):
                    pe.wait_ge(normed, phase + t + 1)
                else:
                    pe.wait_ge(gated, 2 * (phase - 1) + 2 * half + t + 1)
                bank_free(pe, JOB["batch", b])
                for j in range(4):
                    c = half * NCOL + j * P
                    last = nc.tensor.transpose(tp[JOB["batch", b] % 2][:, j * P:(j + 1) * P],
                                               act_src[:, t, c:c + P], ident[:])
                last.then_inc(turned, 1)

            pe.wait_ge(const_done, 4)
            for n in range(N_SLOTS):
                for i in TURN_AT.get(n, []):
                    turn_qk(i)
                if n - 1 in STEP_AT:
                    turn_probs(STEP_AT[n - 1])
                if n in STEP_AT:
                    scores(STEP_AT[n])
                for b in BATCH_AT.get(n, []):
                    turn_batch(b)
                if n - 2 in STEP_AT:
                    values(STEP_AT[n - 2])
                project(n)

        @block.vector
        def _(dve):
            steps = [0]

            def chain(ins):
                steps[0] += 1
                ins.then_inc(dve_chain, 1)
                dve.wait_ge(dve_chain, steps[0])

            def split_lo(p):
                dve.wait_ge(hi_done, p + 1)
                nc.vector.tensor_tensor(w_lo[:, p % RING, :], raw[:, p // PER_DMA % RAW, p % PER_DMA, :],
                                        w_hi[:, p % RING, :].bitcast(F32), ALU.subtract).then_inc(lo_done, 1)

            def norm(i):
                t = i % 2
                dve.wait_ge(rstd_done, i + 1)
                dve.wait_ge(gains_in, 16)
                if i >= 2:
                    dve.wait_ge(turned, BATCH[1, t, 1] + 1)
                nc.vector.scalar_tensor_tensor(out=act_src[:, t, :], in0=x_sb[:, t, :], scalar=rstd[:, i:i + 1],
                                               in1=gains[:, i // 2, :], op0=ALU.mult,
                                               op1=ALU.mult).then_inc(normed, 1)

            def batch_lo(b):
                _, t, half = BATCHES[b]
                dve.wait_ge(a_hi_done, b + 1)
                cols = slice(t * P, (t + 1) * P)
                nc.vector.tensor_tensor(a_lo[:, 4 * half:4 * half + 4, cols],
                                        tp[JOB["batch", b] % 2][:].rearrange("p (k n) -> p k n", k=4),
                                        a_hi[:, 4 * half:4 * half + 4, cols].bitcast(F32),
                                        ALU.subtract).then_inc(a_lo_done, 1)

            def rotate(u):
                name, t = UNITS[u]
                i, e = QK.index(u), STAGED.index(u)
                n = 2 if name == "kvC" else CH
                kind = {"qA": 0, "kA": 1, "qB": 2, "kB": 3, "qC0": 4, "qC1": 4, "kvC": 5}[name]
                w = n * HD
                dve.wait_ge(staged, e + 1)
                if i >= 2:
                    dve.wait_ge(qk_rstd, i - 1)
                    dve.wait_ge(qk_turned, i - 1)
                if i == 0:
                    dve.wait_ge(const_done, 8)
                nc.vector.tensor_reduce(msq[:, i % 2, 0:n],
                                        stage2[:, e % 2, 0:w].rearrange("p (h d) -> p h d", h=n),
                                        AX_X, ALU.add).then_inc(msq_done, 1)
                if i >= 1:
                    dve.wait_ge(rotated, i)
                src = stage[:, e % 2, 0:w]
                nc.vector.tensor_tensor(rot_a[:, 0:w].rearrange("p (h d) -> p h d", h=n),
                                        src.rearrange("p (h d) -> p h d", h=n),
                                        rope_c[:, t, kind:kind + 1, :].to_broadcast([P, n, HD]), ALU.mult)
                swapped = src.rearrange("p (h s d) -> p h s d", h=n, s=2)[:, :, ::-1, :]
                table = rope_s[:, t, kind:kind + 1, :].rearrange("p h (s d) -> p h s d", s=2)
                chain(nc.vector.tensor_tensor(rot_b[:, 0:w].rearrange("p (h s d) -> p h s d", h=n, s=2),
                                              swapped, table.to_broadcast([P, n, 2, HD // 2]), ALU.mult))
                if name[0] == "q":
                    nc.vector.tensor_tensor(rot[:, i % 2, 0:w], rot_a[:, 0:w], rot_b[:, 0:w],
                                            ALU.add).then_inc(rotated, 1)
                else:
                    chain(nc.vector.tensor_tensor(rot_a[:, 0:w], rot_a[:, 0:w], rot_b[:, 0:w], ALU.add))
                    dve.wait_ge(qk_rstd, i + 1)
                    nc.vector.tensor_tensor(rot[:, i % 2, 0:w].rearrange("p (h d) -> p h d", h=n),
                                            rot_a[:, 0:w].rearrange("p (h d) -> p h d", h=n),
                                            r_key[:, i % 2, 0:n].rearrange("p (h o) -> p h o", o=1).to_broadcast([P, n, HD]),
                                            ALU.mult).then_inc(rotated, 1)

            def silu(u):
                name, t = UNITS[u]
                e, half = STAGED.index(u), ["zA", "zB", "zC0", "zC1"].index(name) % 2
                dve.wait_ge(staged, e + 1)
                dve.wait_ge(turned, BATCH[0 if name in ("zA", "zB") else 2, t, 1] + 1)
                nc.vector.scalar_tensor_tensor(out=act_src[:, t, half * NCOL:(half + 1) * NCOL],
                                               in0=stage2[:, e % 2, :], scalar=1.0, in1=stage[:, e % 2, :],
                                               op0=ALU.add, op1=ALU.mult).then_inc(silu_done, 1)

            def gate(layer, t, half):
                heads = slice(half * CH, (half + 1) * CH)
                done = (CH * (half + 1) if layer == 0 else HC + CH * (half + 1))
                dve.wait_ge(head_copied, done)
                l2 = y[:, t, heads, HD]
                if layer == 1:
                    dve.wait_ge(sinks_exp, half + 1)
                    chain(nc.vector.scalar_tensor_tensor(out=inv_l[:, t, heads], in0=sink_e[:, heads, t], scalar=2.0,
                                                         in1=l2, op0=ALU.mult, op1=ALU.add))
                    l2 = inv_l[:, t, heads]
                chain(nc.vector.reciprocal(inv_l[:, t, heads], l2))
                chain(nc.vector.tensor_tensor(y[:, t, heads, 0:HD], y[:, t, heads, 0:HD],
                                              inv_l[:, t, heads].rearrange("p (h o) -> p h o", o=1).to_broadcast([P, CH, HD]), ALU.mult))
                g = act_src[:, t, half * NCOL:(half + 1) * NCOL].rearrange("p (h d) -> p h d", h=CH)
                dve.wait_ge(silu_done, ZU.index(UNIT[[["zA", "zB"], ["zC0", "zC1"]][layer][half], t]) + 1)
                nc.vector.tensor_tensor(g, g, y[:, t, heads, 0:HD], ALU.mult).then_inc(gated, 1)

            def mask(s):
                mixer, h = STEPS[s]
                c = s if s < HC else s - HC
                m = masks[:, "ABC".index(mixer), :]
                need = mixer if mixer != "C" else f"C{h // CH}"
                dve.wait_ge(scores_done, s + 1)
                dve.wait_ge(qk_rstd, SCORES_NEED[need] + 1)
                if s >= 2:
                    dve.wait_ge(probs_turned, s - 1)
                first = BIG if mixer != "C" else neg_sinks[:, h:h + 1]
                for t, cols, mk in ((0, slice(0, P), m[:, P:2 * P]), (1, slice(P, 3 * P), m)):
                    last = nc.vector.tensor_tensor_reduce(out=probs[:, s % 2, cols], in0=sc[s % 2][:, cols], in1=mk,
                                                          scale=query_scale(mixer, h, t), scalar=first,
                                                          op0=ALU.add, op1=ALU.min, accum_out=neg_m[:, c, t:t + 1])
                last.then_inc(masked, 1)

            def copy_head(s):
                c = s if s < HC else s - HC
                dve.wait_ge(head_done, s + 1)
                if s >= HC:
                    dve.wait_ge(gated, 4)
                nc.vector.tensor_copy(y[:, :, c, :], ob[s % 2][:, 0:2 * VW].rearrange("p (t d) -> p t d", t=T)
                                      ).then_inc(head_copied, 1)

            def add_residual(u):
                name, t = UNITS[u]
                c = int(name[1]) * NCOL
                dve.wait_ge(proj_done, u + 1)
                if name[0] == "p":
                    dve.wait_ge(normed, 4)
                nc.vector.tensor_tensor(x_sb[:, t, c:c + NCOL], x_sb[:, t, c:c + NCOL], acc[u % 2][:],
                                        ALU.add).then_inc(out_added, 1)

            def add_sinks(g):
                heads = slice(g * CH, (g + 1) * CH)
                dve.wait_ge(masked, HC + (g + 1) * CH)
                nc.vector.tensor_tensor(sink_e[:, heads, :], neg_m[:, heads, :],
                                        sinks[:, heads].rearrange("p (h o) -> p h o", o=1).to_broadcast([P, CH, T]),
                                        ALU.add).then_inc(sinks_added, 1)

            norm(0)
            norm(1)
            for p in SPLIT_AT[-1]:
                split_lo(p)
            for b in BATCH_AT[0]:
                batch_lo(b)
            dve.wait_ge(masks_in, 48)
            chain(nc.vector.tensor_scalar(neg_sinks[:], sinks[:], -1.0, None, ALU.mult))
            GATES = {}
            for t in range(T):
                GATES.setdefault(BEGIN[UNIT["zB", 1]], []).append((0, t, 0))
                GATES.setdefault(END[UNIT["zB", 1]] + 2, []).append((0, t, 1))
                GATES.setdefault(BEGIN[UNIT["zC1", 1]] + t, []).append((1, t, 0))
                GATES.setdefault(END[UNIT["zC1", 1]] + 3, []).append((1, t, 1))
            for n in range(N_SLOTS):
                if n in STEP_AT:
                    mask(STEP_AT[n])
                if n - 2 in STEP_AT:
                    copy_head(STEP_AT[n - 2])
                for layer, t, half in GATES.get(n, []):
                    gate(layer, t, half)
                if n > 0:
                    for b in BATCH_AT.get(n, []):
                        batch_lo(b)
                for u in range(len(UNITS)):
                    if n == END[u] + 1:
                        if u in QK:
                            rotate(u)
                        elif u in ZU:
                            silu(u)
                        elif is_out(u):
                            add_residual(u)
                for t in range(T):
                    if n == END[UNIT["o1", t]] + 2:
                        norm(2 + t)
                if n - 1 in STEP_AT and STEP_AT[n - 1] in (HC + CH - 1, N_STEPS - 1):
                    add_sinks(int(STEP_AT[n - 1] == N_STEPS - 1))
                for p in SPLIT_AT[n]:
                    split_lo(p)
            for u in OUTS:
                if END[u] + 1 >= N_SLOTS:
                    add_residual(u)


def packed_weights(even_in, even_out, odd_in, odd_out):
    heads = np.array([p // 2 + 8 * (p % 2) for p in range(HC)])
    cols = (heads[:, None] * HD + np.arange(HD)[None, :]).reshape(-1)
    width = HC * HD
    cut = {}
    for i, n in enumerate(("qA", "kA", "vA", "zA", "qB", "kB", "vB", "zB")):
        cut[n] = even_in[:, i * NCOL:(i + 1) * NCOL]
    q, kv, z = odd_in[:, 0:width][:, cols], odd_in[:, width:width + 256], odd_in[:, width + 256:][:, cols]
    out = odd_out[cols, :]
    cut["kvC"] = kv
    for i in range(2):
        half = slice(i * NCOL, (i + 1) * NCOL)
        cut[f"o{i}"], cut[f"qC{i}"], cut[f"zC{i}"], cut[f"p{i}"] = even_out[:, half], q[:, half], z[:, half], out[:, half]
    rows = []
    for name, w in CHUNKS:
        c = cut[name].reshape(K, P, w).transpose(1, 0, 2).reshape(P, -1, PER_DMA * PIECE)
        rows.append(c.transpose(1, 0, 2))
    return np.ascontiguousarray(np.concatenate(rows)), heads


def tables():
    inv = np.float32(ROPE_THETA) ** (-np.arange(0, HD, 2, dtype=np.float32) / np.float32(HD))
    ang = np.arange(S, dtype=np.float32)[:, None] * inv[None, :].astype(np.float32)
    cos, sin = np.cos(ang), np.sin(ang)
    i = np.arange(P)[:, None]
    dist = np.concatenate([P + i - np.arange(P)[None, :], i - np.arange(P)[None, :]], axis=1)
    count = sum(((dist >= 0) & (dist <= w) & (dist % d == 0)).astype(np.float32)
                for w, d in ((128, 1), (512, 4), (2048, 16)))
    keep = [count > 0, dist >= 0, (dist >= 0) & (dist < WINDOW)]
    m = np.stack([np.where(k, 0.0, NEG) for k in keep] + [count], axis=1).astype(np.float32)
    return (np.concatenate([cos, cos], axis=1).astype(np.float32),
            np.concatenate([-sin, sin], axis=1).astype(np.float32), np.ascontiguousarray(m))


def kernel(**inputs):
    import concourse.bacc as bacc
    from concourse.bass_utils import run_bass_kernel_spmd as run

    a = {k: np.asarray(v) for k, v in inputs.items()}
    w, heads = packed_weights(a["w_in_even"][0], a["w_out_even"][0], a["w_in_odd"][0], a["w_out_odd"][0])
    g = [a[k][0] for k in ("qnorm_a", "knorm_a", "qnorm_b", "knorm_b", "qnorm_c", "knorm_c")]
    swapped = [np.concatenate([v[HD // 2:], v[:HD // 2]]) for v in g]
    cos, sin, masks = tables()
    arrays = {
        "x": a["x"][0],
        "w": w,
        "gains": np.concatenate([a["norm_even"][0], a["norm_odd"][0]])[None, :],
        "heads": np.concatenate(g + swapped)[None, :],
        "cos": cos,
        "sin": sin,
        "masks": masks,
        "sinks": a["sinks_c"][0][heads][None, :],
    }
    arrays = {k: np.ascontiguousarray(v) for k, v in arrays.items()}
    nc = bacc.Bacc("TRN2", target_bir_lowering=False, num_devices=1)
    args = [nc.dram_tensor(f"in_{k}", v.shape, mybir.dt.from_np(v.dtype), kind="ExternalInput").ap()
            for k, v in arrays.items()]
    out = nc.dram_tensor("out", (S, D), F32, kind="ExternalOutput").ap()
    bass_hybrid_dilated_moba_swa_sink_trunk(nc, *args, out)
    got = run(nc, [{f"in_{k}": v for k, v in arrays.items()}], core_ids=[0])
    return got.results[0]["out"].reshape(1, S, D)
```

```python
from contextlib import ExitStack

import numpy as np

import concourse.bass as bass
from concourse import mybir

F32 = mybir.dt.float32
F32R = mybir.dt.float32r
ALU = mybir.AluOpType
ACT = mybir.ActivationFunctionType
AX_X = mybir.AxisListType.X

P = 128
S = 256
T = S // P
D = 1024
K = D // P
HD = 64
HA = 8
HC = 16
NCOL = 512
CH = NCOL // HD
VW = HD + 1
EPS = 1e-6
NEG = -1e30
BIG = 3e38
ROPE_THETA = 10000.0
WINDOW = 128

CHUNKS = ([(n, NCOL) for n in ("qA", "kA", "vA", "qB", "kB", "vB", "zA", "zB", "o0", "o1")]
          + [("kvC", 256)] + [(n, NCOL) for n in ("qC0", "qC1", "zC0", "zC1", "p0", "p1")])
CHUNK = {n: i for i, (n, _) in enumerate(CHUNKS)}
PIECE = 1024
KPP = [PIECE // w for _, w in CHUNKS]
PIECES = [K // kpp for kpp in KPP]
FIRST_PIECE = [sum(PIECES[:i]) for i in range(len(CHUNKS))]
N_PIECES = sum(PIECES)
PER_DMA = 2
N_DMAS = N_PIECES // PER_DMA
RAW = 3
RING = 9

UNITS = [(c, t) for c in ("qA", "kA", "vA", "qB", "kB", "vB", "zA", "zB") for t in range(T)]
UNITS += [("o0", 0), ("o1", 0), ("o0", 1), ("o1", 1)]
UNITS += [("kvC", 0), ("qC0", 0), ("kvC", 1), ("qC0", 1), ("qC1", 0), ("qC1", 1)]
UNITS += [("zC0", 0), ("zC0", 1), ("zC1", 0), ("zC1", 1)]
UNITS += [("p0", 0), ("p1", 0), ("p0", 1), ("p1", 1)]
UNIT = {u: i for i, u in enumerate(UNITS)}


def is_out(u):
    return UNITS[u][0][0] in "op"


QK = [u for u, (c, _) in enumerate(UNITS) if c[0] in "qk"]
ZU = [u for u, (c, _) in enumerate(UNITS) if c[0] == "z"]
VU = [u for u, (c, _) in enumerate(UNITS) if c[0] == "v"]
STAGED = [u for u in range(len(UNITS)) if u in QK or u in ZU]
PROJ = [u for u in range(len(UNITS)) if not is_out(u)]
OUTS = [u for u in range(len(UNITS)) if is_out(u)]

PARTS = {"q": 2, "k": 2, "v": 2, "z": 2, "o": 2, "p": 2, "kvC": 1, "qC0": 2, "qC1": 4, "zC0": 4, "zC1": 4}
SLOTS = []
for _u, (_c, _t) in enumerate(UNITS):
    _n = PARTS[_c] if _c in PARTS else PARTS[_c[0]]
    if _c in ("o0", "p0") and _t == 0:
        SLOTS += [(_u + j, i, _n) for i in range(_n) for j in range(2)]
    elif not (_c in ("o1", "p1") and _t == 0):
        SLOTS += [(_u, i, _n) for i in range(_n)]
N_SLOTS = len(SLOTS)
BEGIN = {u: min(n for n, s in enumerate(SLOTS) if s[0] == u) for u in range(len(UNITS))}
END = {u: max(n for n, s in enumerate(SLOTS) if s[0] == u) for u in range(len(UNITS))}


def end(chunk, t):
    return END[UNIT[chunk, t]]


STEPS = [("A", h) for h in range(HA)] + [("B", h) for h in range(HA)] + [("C", h) for h in range(HC)]
N_STEPS = len(STEPS)
SCORE_SLOTS = [end("kA", 1) + d for d in (4, 5, 7, 8, 10, 11, 13, 14)]
SCORE_SLOTS += [end("kB", 1) + 4 + d for d in range(HA)]
SCORE_SLOTS += [end("qC0", 1) + 6 + d for d in range(HC)]
TURN_SLOTS = [n + (2 if STEPS[s][0] == "C" else 1) for s, n in enumerate(SCORE_SLOTS)]
STEP_AT = {n: s for s, n in enumerate(SCORE_SLOTS)}
PROBS_AT = {n: s for s, n in enumerate(TURN_SLOTS)}
VALUE_AT = {n + 1: s for s, n in enumerate(TURN_SLOTS)}
assert len(STEP_AT) == len(PROBS_AT) == N_STEPS
PROBS = 3

TURN_AT = {}
for _i, _u in enumerate(QK):
    TURN_AT.setdefault(END[_u] + (5 if UNITS[_u] == ("qC0", 1) else 3), []).append(_i)

BATCHES = [(phase, t, half) for phase in range(4) for t in range(T) for half in range(2)]
BATCH = {b: i for i, b in enumerate(BATCHES)}
BATCH_AT = {0: [(0, 0, 0), (0, 0, 1)], 1: [(0, 1, 0), (0, 1, 1)],
            end("zB", 0) + 1: [(1, 0, 0)],
            end("zB", 1) + 3: [(1, 0, 1)], end("zB", 1) + 4: [(1, 1, 0), (1, 1, 1)],
            BEGIN[UNIT["o1", 1]]: [(2, 0, 0), (2, 0, 1)],
            BEGIN[UNIT["kvC", 1]] - 1: [(2, 1, 0), (2, 1, 1)],
            end("zC1", 0) + 2: [(3, 0, 0)],
            end("zC1", 1) + 3: [(3, 0, 1)], end("zC1", 1) + 4: [(3, 1, 0), (3, 1, 1)]}
BATCH_AT = {n: [BATCH[b] for b in bs] for n, bs in BATCH_AT.items()}
GATE_AT = {BEGIN[UNIT["zB", 0]]: [(0, 0, 0)], BEGIN[UNIT["zB", 0]] + 1: [(0, 1, 0)],
           end("zB", 1) + 2: [(0, 0, 1), (0, 1, 1)],
           end("zC0", 1) + 1: [(1, 0, 0)], end("zC0", 1) + 2: [(1, 1, 0)],
           end("zC1", 1) + 1: [(1, 0, 1), (1, 1, 1)]}
GATES = [g for n in sorted(GATE_AT) for g in GATE_AT[n]]

JOBS = []
for _n in range(N_SLOTS):
    JOBS += [("turn", i) for i in TURN_AT.get(_n, [])]
    JOBS += [("probs", PROBS_AT[_n])] if _n in PROBS_AT else []
    JOBS += [("batch", b) for b in BATCH_AT.get(_n, [])]
JOB = {j: i for i, j in enumerate(JOBS)}


def last_use(piece):
    c = max(i for i in range(len(CHUNKS)) if FIRST_PIECE[i] <= piece)
    return max(UNIT[CHUNKS[c][0], t] for t in range(T))


def split_slots():
    out = {-1: list(range(5))}
    p = 5
    for n in range(N_SLOTS):
        out[n] = []
        while p < N_PIECES and (p < RING or END[last_use(p - RING)] < n):
            c = max(i for i in range(len(CHUNKS)) if FIRST_PIECE[i] <= p)
            use = min(BEGIN[UNIT[CHUNKS[c][0], t]] for t in range(T))
            if len(out[n]) >= (1 if use > n + 2 else 2):
                break
            out[n].append(p)
            p += 1
    assert p == N_PIECES
    return out


SPLIT_AT = split_slots()


def bass_hybrid_dilated_moba_swa_sink_trunk(nc, x_d, w_d, gains_d, heads_d, cos_d, sin_d, masks_d, sinks_d, out_d):
    with ExitStack() as ctx:
        def sb(name, shape, dt=F32):
            return ctx.enter_context(nc.sbuf_tensor(name, shape, dt))

        def pb(name):
            return ctx.enter_context(nc.psum_tensor(name, [P, 512], F32))

        def sem(name):
            return ctx.enter_context(nc.semaphore(name))

        x_sb = sb("x_sb", [P, T, D])
        gains = sb("gains", [P, D])
        head_g = sb("head_g", [P, 2, 6, HD])
        cos_sb = sb("cos_sb", [P, T, HD])
        sin_sb = sb("sin_sb", [P, T, HD])
        rope_c = sb("rope_c", [P, T, 6, HD])
        rope_s = sb("rope_s", [P, T, 6, HD])
        masks = sb("masks", [P, 3, 2 * P])
        count_t = sb("count_t", [P, 3 * P])
        sinks = sb("sinks", [P, HC])
        neg_sinks = sb("neg_sinks", [P, HC])
        ident = sb("ident", [P, P])
        minus_half = sb("minus_half", [P, CH])
        raw = sb("raw", [P, RAW, PER_DMA, PIECE])
        w_hi = sb("w_hi", [P, RING, PIECE], F32R)
        w_lo = sb("w_lo", [P, RING, PIECE], F32R)
        a_hi = sb("a_hi", [P, K, S], F32R)
        a_lo = sb("a_lo", [P, K, S], F32R)
        act_src = sb("act_src", [P, T, D])
        stage = sb("stage", [P, 2, NCOL])
        stage2 = sb("stage2", [P, 2, NCOL])
        rot_a = sb("rot_a", [P, NCOL])
        rot_b = sb("rot_b", [P, NCOL])
        rot = sb("rot", [P, 2, NCOL])
        msq = sb("msq", [P, 2, CH])
        r_tmp = sb("r_tmp", [P, 2, CH])
        r_key = sb("r_key", [P, 2, CH])
        r_qry = sb("r_qry", [P, 8, CH])
        qk_t = sb("qk_t", [P, 16, S])
        kc_t = sb("kc_t", [P, S])
        va = sb("va", [P, T, HA, VW])
        vb = sb("vb", [P, T, HA, VW])
        vc = sb("vc", [P, T, 2, VW])
        probs = sb("probs", [P, PROBS, 3 * P])
        probs_t = sb("probs_t", [P, 2, 3 * P])
        neg_m = sb("neg_m", [P, HC, T])
        y = sb("y", [P, T, HC, VW])
        inv_l = sb("inv_l", [P, HC, T])
        sink_e = sb("sink_e", [P, HC, T])
        ssq = sb("ssq", [P, 4, 2])
        ms = sb("ms", [P, 4])
        rstd = sb("rstd", [P, 4])
        half_rstd = sb("half_rstd", [P, 4])

        acc = [pb(f"acc{i}") for i in range(2)]
        sc = [pb(f"sc{i}") for i in range(2)]
        tp = [pb(f"tp{i}") for i in range(2)]
        ob = [pb(f"ob{i}") for i in range(2)]

        x_in = [sem(f"x_in{t}") for t in range(T)]
        gain_in = [sem(f"gain_in{i}") for i in range(2)]
        gain_done = sem("gain_done")
        heads_in = sem("heads_in")
        tables_in = sem("tables_in")
        masks_in = sem("masks_in")
        first_in = sem("first_in")
        raw_in = [sem(f"raw_in{i}") for i in range(RAW)]
        hi_done = sem("hi_done")
        lo_done = sem("lo_done")
        const_done = sem("const_done")
        gp_chain = sem("gp_chain")
        dve_chain = sem("dve_chain")
        sumsq_done = sem("sumsq_done")
        rstd_done = sem("rstd_done")
        normed = sem("normed")
        turned = sem("turned")
        a_hi_done = sem("a_hi_done")
        a_lo_done = sem("a_lo_done")
        proj_done = sem("proj_done")
        out_added = sem("out_added")
        staged = sem("staged")
        msq_done = sem("msq_done")
        qk_rstd = sem("qk_rstd")
        rotated = sem("rotated")
        silu_done = sem("silu_done")
        qk_turned = sem("qk_turned")
        qk_ready = sem("qk_ready")
        v_ready = sem("v_ready")
        scores_done = sem("scores_done")
        masked = sem("masked")
        exp_done = sem("exp_done")
        probs_turned = sem("probs_turned")
        probs_counted = sem("probs_counted")
        probs_copied = sem("probs_copied")
        head_done = sem("head_done")
        head_copied = sem("head_copied")
        sink_done = sem("sink_done")
        gated = sem("gated")
        stored = sem("stored")

        y_flat = y[:].rearrange("p t h d -> p (t h d)")

        block = ctx.enter_context(nc.Block())

        def parts_of(name):
            c = CHUNK[name]
            return CHUNKS[c][1], KPP[c], FIRST_PIECE[c]

        def probs_in_sbuf(eng, s):
            if s < HA:
                eng.wait_ge(probs_counted, s + 1)
            else:
                eng.wait_ge(probs_copied, s - HA + 1)

        def bank_free(eng, j):
            if j >= 2:
                kind, i = JOBS[j - 2]
                if kind == "turn":
                    eng.wait_ge(qk_ready, i + 1)
                elif kind == "probs":
                    probs_in_sbuf(eng, i)
                else:
                    eng.wait_ge(a_lo_done, i + 1)

        def query_scale(mixer, h, t):
            col = {"A": 0, "B": 2, "C": 4 + 2 * (h // CH)}[mixer] + t
            return r_qry[:, col, h % CH:h % CH + 1]

        def q_of(mixer, h):
            side = HD * (h % 2)
            return qk_t[side:side + HD, {"A": 0, "B": 8, "C": 0}[mixer] + h // 2, :]

        def k_of(mixer, h):
            side = HD * (h % 2)
            if mixer == "C":
                return kc_t[side:side + HD, :]
            return qk_t[side:side + HD, {"A": 4, "B": 12}[mixer] + h // 2, :]

        def v_of(mixer, h, t):
            if mixer == "C":
                return vc[:, t, h % 2, :]
            return (va if mixer == "A" else vb)[:, t, h, :]

        SCORES_NEED = {"A": QK.index(UNIT["kA", 1]), "B": QK.index(UNIT["kB", 1]),
                       "C0": QK.index(UNIT["qC0", 1]), "C1": QK.index(UNIT["qC1", 1])}

        @block.sync
        def _(sp):
            sp.dma_start(y_flat[0:1, 0:D], gains_d[:, 0:D]).then_inc(gain_in[0], 16)
            sp.dma_start(x_sb[:, 0, :], x_d[0:P, :]).then_inc(x_in[0], 16)
            sp.dma_start(raw[:, 0, 0, :], w_d[0, :, 0:PIECE]).then_inc(first_in, 16)
            sp.dma_start(x_sb[:, 1, :], x_d[P:S, :]).then_inc(x_in[1], 16)
            sp.dma_start(raw[:, 0, 1, :], w_d[0, :, PIECE:2 * PIECE]).then_inc(raw_in[0], 16)
            for d in range(1, N_DMAS):
                if d >= RAW:
                    sp.wait_ge(lo_done, PER_DMA * (d - RAW + 1))
                sp.dma_start(raw[:, d % RAW, :, :].rearrange("p a n -> p (a n)"),
                             w_d[d, :, :]).then_inc(raw_in[d % RAW], 16)
                if d == 1:
                    sp.dma_start(y_flat[0:1, D:D + 12 * HD], heads_d).then_inc(heads_in, 16)
                    sp.dma_start(cos_sb[:], cos_d.rearrange("(t p) n -> p t n", p=P)).then_inc(tables_in, 16)
                    sp.dma_start(sin_sb[:], sin_d.rearrange("(t p) n -> p t n", p=P)).then_inc(tables_in, 16)
                if d == 3:
                    sp.dma_start(masks[:], masks_d[:, 0:6 * P].rearrange("p (m n) -> p m n", m=3)
                                 ).then_inc(masks_in, 16)
                    sp.dma_start(count_t[:], masks_d[:, 6 * P:9 * P]).then_inc(masks_in, 16)
                    sp.dma_start(sinks[:], sinks_d.to_broadcast([P, HC])).then_inc(masks_in, 16)
                if d == 4:
                    sp.wait_ge(normed, 4)
                    sp.dma_start(gains[:], gains_d[:, D:2 * D].to_broadcast([P, D])).then_inc(gain_in[1], 16)
            for i, u in enumerate(OUTS[4:]):
                name, t = UNITS[u]
                c = int(name[1]) * NCOL
                sp.wait_ge(out_added, 4 + i + 1)
                sp.dma_start(out_d[t * P:(t + 1) * P, c:c + NCOL], x_sb[:, t, c:c + NCOL]).then_inc(stored, 16)
            sp.wait_ge(stored, 16 * 4)

        @block.gpsimd
        def _(pool):
            steps = [0]

            def chain(ins):
                steps[0] += 1
                ins.then_inc(gp_chain, 1)
                pool.wait_ge(gp_chain, steps[0])

            chain(nc.gpsimd.memset(minus_half[:], -0.5))
            chain(nc.gpsimd.memset(ident[:], 0.0))
            pool.wait_ge(gain_in[0], 16)
            nc.gpsimd.partition_broadcast(gains[:], y_flat[0:1, 0:D], P).then_inc(gain_done, 1)
            nc.gpsimd.affine_select(out=ident[:], in_=ident[:], compare_op=ALU.not_equal, fill=1.0, base=0,
                                    pattern=[[-1, P]], channel_multiplier=1).then_inc(const_done, 1)
            for v in (va, vb, vc):
                nc.gpsimd.memset(v[:, :, :, HD:VW], 2.0).then_inc(const_done, 1)

            def row_norm(i):
                pool.wait_ge(sumsq_done, 2 * (i + 1))
                chain(nc.gpsimd.tensor_tensor(ms[:, i:i + 1], ssq[:, i, 0:1], ssq[:, i, 1:2], ALU.add))
                chain(nc.gpsimd.tensor_scalar(ms[:, i:i + 1], ms[:, i:i + 1], 1.0 / D, EPS, ALU.mult, ALU.add))
                chain(nc.gpsimd.tensor_tensor(rstd[:, i:i + 1], ms[:, i:i + 1], minus_half[:, 0:1], ALU.pow))
                nc.gpsimd.tensor_scalar(half_rstd[:, i:i + 1], rstd[:, i:i + 1], 0.5, None,
                                        ALU.mult).then_inc(rstd_done, 1)

            def head_norm(i):
                u = QK[i]
                name, t = UNITS[u]
                n = 2 if name == "kvC" else CH
                pool.wait_ge(msq_done, i + 1)
                if i >= 2:
                    pool.wait_ge(rotated, i - 1)
                    pool.wait_ge(qk_rstd, i - 1)
                chain(nc.gpsimd.tensor_scalar(r_tmp[:, i % 2, 0:n], msq[:, i % 2, 0:n], 1.0 / HD, EPS,
                                              ALU.mult, ALU.add))
                if name[0] == "k":
                    nc.gpsimd.tensor_tensor(r_key[:, i % 2, 0:n], r_tmp[:, i % 2, 0:n], minus_half[:, 0:n],
                                            ALU.pow).then_inc(qk_rstd, 1)
                else:
                    col = {"qA": 0, "qB": 2, "qC0": 4, "qC1": 6}[name] + t
                    chain(nc.gpsimd.tensor_tensor(r_qry[:, col, :], r_tmp[:, i % 2, :], minus_half[:], ALU.pow))
                    nc.gpsimd.tensor_scalar(r_qry[:, col, :], r_qry[:, col, :], -float(HD) ** -0.5, None,
                                            ALU.mult).then_inc(qk_rstd, 1)

            row_norm(0)
            row_norm(1)
            pool.wait_ge(heads_in, 16)
            chain(nc.gpsimd.partition_broadcast(head_g[:].rearrange("p a b n -> p (a b n)"),
                                                y_flat[0:1, D:D + 12 * HD], P))
            pool.wait_ge(tables_in, 32)
            for t in range(T):
                for dst, src, g in ((rope_c, cos_sb, 0), (rope_s, sin_sb, 1)):
                    nc.gpsimd.tensor_tensor(dst[:, t, :, :], head_g[:, g, :, :],
                                            src[:, t:t + 1, :].to_broadcast([P, 6, HD]),
                                            ALU.mult).then_inc(const_done, 1)
            qk_end = {}
            for i, u in enumerate(QK):
                qk_end.setdefault(END[u] + 1, []).append(i)
            for n in range(N_SLOTS):
                for i in qk_end.get(n, []):
                    head_norm(i)
                for t in range(T):
                    if n == END[UNIT["o1", t]] + 1:
                        row_norm(2 + t)

        @block.scalar
        def _(act):
            def sum_squares(i, half):
                t = i % 2
                if half == 0 and i < 2:
                    act.wait_ge(x_in[t], 16)
                n = 2 * i + half
                if n >= 1:
                    act.wait_ge(sumsq_done, n)
                if i >= 2:
                    act.wait_ge(head_copied, HC)
                nc.scalar.activation(ob[0][:], x_sb[:, t, half * NCOL:(half + 1) * NCOL], ACT.Square,
                                     accum_out=ssq[:, i, half:half + 1]).then_inc(sumsq_done, 1)

            def split_hi(p):
                d = p // PER_DMA
                if p == 0:
                    act.wait_ge(first_in, 16)
                else:
                    act.wait_ge(raw_in[d % RAW], 16 * (d // RAW + 1))
                if p >= RING:
                    act.wait_ge(proj_done, last_use(p - RING) + 1)
                nc.scalar.activation(w_hi[:, p % RING, :], raw[:, d % RAW, p % PER_DMA, :],
                                     ACT.Copy).then_inc(hi_done, 1)

            def batch_hi(b):
                phase, t, half = BATCHES[b]
                act.wait_ge(turned, b + 1)
                if phase > 0:
                    before = {1: UNIT["zB", t], 2: UNIT["o1", t], 3: UNIT["zC1", t]}[phase]
                    act.wait_ge(proj_done, before + 1)
                nc.scalar.activation(a_hi[:, 4 * half:4 * half + 4, t * P:(t + 1) * P],
                                     tp[JOB["batch", b] % 2][:].rearrange("p (k n) -> p k n", k=4),
                                     ACT.Copy).then_inc(a_hi_done, 1)

            def read_unit(u):
                name, t = UNITS[u]
                act.wait_ge(proj_done, u + 1)
                bank = acc[u % 2]
                row = 2 * int(u > UNIT["o1", 1]) + t
                act.wait_ge(rstd_done, row + 1)
                scale, half_scale = rstd[:, row:row + 1], half_rstd[:, row:row + 1]
                if u in STAGED:
                    e = STAGED.index(u)
                    if e >= 2:
                        former = STAGED[e - 2]
                        if former in QK:
                            act.wait_ge(rotated, QK.index(former) + 1)
                        else:
                            act.wait_ge(silu_done, ZU.index(former) + 1)
                    width = 2 * HD if name == "kvC" else NCOL
                    nc.scalar.activation(stage[:, e % 2, 0:width], bank[:, 0:width], ACT.Copy, scale=scale)
                    if name == "kvC":
                        nc.scalar.activation(vc[:, t, :, 0:HD],
                                             bank[:, width:2 * width].rearrange("p (h d) -> p h d", h=2),
                                             ACT.Copy, scale=scale).then_inc(v_ready, 1)
                    fn, scale = (ACT.Tanh, half_scale) if name[0] == "z" else (ACT.Square, scale)
                    nc.scalar.activation(stage2[:, e % 2, 0:width], bank[:, 0:width], fn,
                                         scale=scale).then_inc(staged, 1)
                else:
                    v = va if name == "vA" else vb
                    nc.scalar.activation(v[:, t, :, 0:HD], bank[:].rearrange("p (h d) -> p h d", h=HA),
                                         ACT.Copy, scale=scale).then_inc(v_ready, 1)

            def copy_turned(i):
                name, t = UNITS[QK[i]]
                act.wait_ge(qk_turned, i + 1)
                cols = slice(t * P, (t + 1) * P)
                bank = tp[JOB["turn", i] % 2]
                if name == "kvC":
                    nc.scalar.activation(kc_t[:, cols], bank[:, 0:P], ACT.Copy).then_inc(qk_ready, 1)
                else:
                    at = {"qA": 0, "kA": 4, "qB": 8, "kB": 12, "qC0": 0, "qC1": 4}[name]
                    if name[1] == "C":
                        act.wait_ge(scores_done, HA)
                    nc.scalar.activation(qk_t[:, at:at + 4, cols], bank[:].rearrange("p (k n) -> p k n", k=4),
                                         ACT.Copy).then_inc(qk_ready, 1)

            def softmax_exp(s):
                act.wait_ge(masked, s + 1)
                c = s if s < HC else s - HC
                for t, cols in ((0, slice(0, P)), (1, slice(P, 3 * P))):
                    last = nc.scalar.activation(probs[:, s % PROBS, cols], probs[:, s % PROBS, cols], ACT.Exp,
                                                bias=neg_m[:, c, t:t + 1], scale=-1.0)
                last.then_inc(exp_done, 1)
                if s >= HC:
                    nc.scalar.activation(sink_e[:, c, :], neg_m[:, c, :], ACT.Exp,
                                         bias=sinks[:, c:c + 1]).then_inc(sink_done, 1)

            def copy_probs(s):
                act.wait_ge(probs_turned, s + 1)
                if s >= 2:
                    act.wait_ge(head_done, s - 1)
                nc.scalar.activation(probs_t[:, s % 2, :], tp[JOB["probs", s] % 2][:, 0:3 * P],
                                     ACT.Copy).then_inc(probs_copied, 1)

            assert SPLIT_AT[-1] == [0, 1, 2, 3, 4]
            batch_hi(0)
            batch_hi(1)
            split_hi(0)
            split_hi(1)
            batch_hi(2)
            batch_hi(3)
            split_hi(2)
            for t in range(T):
                sum_squares(t, 0)
                sum_squares(t, 1)
            split_hi(3)
            split_hi(4)
            for n in range(N_SLOTS):
                for i in TURN_AT.get(n, []):
                    copy_turned(i)
                if n in PROBS_AT and PROBS_AT[n] >= HA:
                    copy_probs(PROBS_AT[n])
                for b in BATCH_AT.get(n, []):
                    if b >= 4:
                        batch_hi(b)
                for u in range(len(UNITS)):
                    if n == END[u] + 1 and not is_out(u):
                        read_unit(u)
                if n in STEP_AT:
                    softmax_exp(STEP_AT[n])
                for t in range(T):
                    for half in range(2):
                        if n == end(f"o{half}", t) + 1:
                            act.wait_ge(out_added, 2 * t + half + 1)
                            sum_squares(2 + t, half)
                for p in SPLIT_AT[n]:
                    split_hi(p)

        @block.tensor
        def _(pe):
            def project(n):
                u, part, parts = SLOTS[n]
                name, t = UNITS[u]
                width, kpp, first = parts_of(name)
                bank = acc[u % 2][:, 0:width]
                phase = 0 if u < UNIT["o0", 0] else 1 if u < UNIT["kvC", 0] else 2 if u < UNIT["p0", 0] else 3
                if part == 0:
                    if u >= 2:
                        if is_out(u - 2):
                            pe.wait_ge(out_added, OUTS.index(u - 2) + 1)
                        elif u - 2 in STAGED:
                            pe.wait_ge(staged, STAGED.index(u - 2) + 1)
                        else:
                            pe.wait_ge(v_ready, VU.index(u - 2) + 1)
                for k in range(K * part // parts, K * (part + 1) // parts):
                    p = first + k // kpp
                    if k % 4 == 0:
                        pe.wait_ge(a_lo_done, BATCH[phase, t, k // 4] + 1)
                    if k % kpp == 0 or k == K * part // parts:
                        pe.wait_ge(lo_done, p + 1)
                    cols = slice((k % kpp) * width, (k % kpp + 1) * width)
                    hi, lo = w_hi[:, p % RING, cols], w_lo[:, p % RING, cols]
                    ah, al = a_hi[:, k, t * P:(t + 1) * P], a_lo[:, k, t * P:(t + 1) * P]
                    nc.tensor.matmul(bank, ah, hi, start=(k == 0), stop=False)
                    nc.tensor.matmul(bank, ah, lo, start=False, stop=False)
                    last = nc.tensor.matmul(bank, al, hi, start=False, stop=(k == K - 1))
                if part == parts - 1:
                    last.then_inc(proj_done, 1)

            def scores(s):
                mixer, h = STEPS[s]
                need = mixer if mixer != "C" else f"C{h // CH}"
                pe.wait_ge(qk_ready, SCORES_NEED[need] + 1)
                if s >= 2:
                    pe.wait_ge(masked, s - 1)
                q, k = q_of(mixer, h), k_of(mixer, h)
                nc.tensor.matmul(sc[s % 2][:, 0:P], q[:, 0:P], k[:, 0:P], start=True, stop=True)
                nc.tensor.matmul(sc[s % 2][:, P:3 * P], q[:, P:2 * P], k[:, 0:2 * P],
                                 start=True, stop=True).then_inc(scores_done, 1)

            def turn_probs(s):
                pe.wait_ge(exp_done, s + 1)
                bank_free(pe, JOB["probs", s])
                for i in range(3):
                    last = nc.tensor.transpose(tp[JOB["probs", s] % 2][:, i * P:(i + 1) * P],
                                               probs[:, s % PROBS, i * P:(i + 1) * P], ident[:])
                last.then_inc(probs_turned, 1)

            def values(s):
                mixer, h = STEPS[s]
                probs_in_sbuf(pe, s)
                pe.wait_ge(v_ready, {"A": 2, "B": 4, "C": 6}[mixer])
                if s >= 2:
                    pe.wait_ge(head_copied, s - 1)
                if s in (0, HC):
                    pe.wait_ge(sumsq_done, 4 if s == 0 else 8)
                pt, o = probs_t[:, s % 2, :], ob[s % 2]
                nc.tensor.matmul(o[:, 0:VW], pt[:, 0:P], v_of(mixer, h, 0), start=True, stop=True)
                nc.tensor.matmul(o[:, VW:2 * VW], pt[:, P:2 * P], v_of(mixer, h, 0), start=True, stop=False)
                nc.tensor.matmul(o[:, VW:2 * VW], pt[:, 2 * P:3 * P], v_of(mixer, h, 1),
                                 start=False, stop=True).then_inc(head_done, 1)

            def turn_qk(i):
                pe.wait_ge(rotated, i + 1)
                bank_free(pe, JOB["turn", i])
                for j in range(1 if UNITS[QK[i]][0] == "kvC" else 4):
                    last = nc.tensor.transpose(tp[JOB["turn", i] % 2][:, j * P:(j + 1) * P],
                                               rot[:, i % 2, j * P:(j + 1) * P], ident[:])
                last.then_inc(qk_turned, 1)

            def turn_batch(b):
                phase, t, half = BATCHES[b]
                if phase in (0, 2):
                    pe.wait_ge(normed, 2 * phase + 2 * t + half + 1)
                else:
                    pe.wait_ge(gated, GATES.index((phase // 2, t, half)) + 1)
                bank_free(pe, JOB["batch", b])
                for j in range(4):
                    c = half * NCOL + j * P
                    last = nc.tensor.transpose(tp[JOB["batch", b] % 2][:, j * P:(j + 1) * P],
                                               act_src[:, t, c:c + P], ident[:])
                last.then_inc(turned, 1)

            pe.wait_ge(const_done, 4)
            for n in range(N_SLOTS):
                for i in TURN_AT.get(n, []):
                    turn_qk(i)
                if n in PROBS_AT:
                    turn_probs(PROBS_AT[n])
                if n in STEP_AT:
                    scores(STEP_AT[n])
                for b in BATCH_AT.get(n, []):
                    turn_batch(b)
                if n in VALUE_AT:
                    values(VALUE_AT[n])
                project(n)

        @block.vector
        def _(dve):
            steps = [0]

            def chain(ins):
                steps[0] += 1
                ins.then_inc(dve_chain, 1)
                dve.wait_ge(dve_chain, steps[0])

            def split_lo(p):
                dve.wait_ge(hi_done, p + 1)
                nc.vector.tensor_tensor(w_lo[:, p % RING, :], raw[:, p // PER_DMA % RAW, p % PER_DMA, :],
                                        w_hi[:, p % RING, :].bitcast(F32), ALU.subtract).then_inc(lo_done, 1)

            def apply_gain(layer, t, half):
                cols = slice(half * NCOL, (half + 1) * NCOL)
                if layer == 0:
                    dve.wait_ge(gain_done, 1)
                    dve.wait_ge(x_in[t], 16)
                else:
                    dve.wait_ge(gain_in[1], 16)
                    dve.wait_ge(out_added, 2 * t + half + 1)
                    dve.wait_ge(turned, BATCH[1, t, 1] + 1)
                nc.vector.tensor_tensor(act_src[:, t, cols], x_sb[:, t, cols], gains[:, cols],
                                        ALU.mult).then_inc(normed, 1)

            def batch_lo(b):
                _, t, half = BATCHES[b]
                dve.wait_ge(a_hi_done, b + 1)
                cols = slice(t * P, (t + 1) * P)
                nc.vector.tensor_tensor(a_lo[:, 4 * half:4 * half + 4, cols],
                                        tp[JOB["batch", b] % 2][:].rearrange("p (k n) -> p k n", k=4),
                                        a_hi[:, 4 * half:4 * half + 4, cols].bitcast(F32),
                                        ALU.subtract).then_inc(a_lo_done, 1)

            def rotate(u):
                name, t = UNITS[u]
                i, e = QK.index(u), STAGED.index(u)
                n = 2 if name == "kvC" else CH
                kind = {"qA": 0, "kA": 1, "qB": 2, "kB": 3, "qC0": 4, "qC1": 4, "kvC": 5}[name]
                w = n * HD
                dve.wait_ge(staged, e + 1)
                if i >= 2:
                    dve.wait_ge(qk_rstd, i - 1)
                    dve.wait_ge(qk_turned, i - 1)
                if i == 0:
                    dve.wait_ge(const_done, 8)
                nc.vector.tensor_reduce(msq[:, i % 2, 0:n],
                                        stage2[:, e % 2, 0:w].rearrange("p (h d) -> p h d", h=n),
                                        AX_X, ALU.add).then_inc(msq_done, 1)
                if i >= 1:
                    dve.wait_ge(rotated, i)
                src = stage[:, e % 2, 0:w]
                nc.vector.tensor_tensor(rot_a[:, 0:w].rearrange("p (h d) -> p h d", h=n),
                                        src.rearrange("p (h d) -> p h d", h=n),
                                        rope_c[:, t, kind:kind + 1, :].to_broadcast([P, n, HD]), ALU.mult)
                swapped = src.rearrange("p (h s d) -> p h s d", h=n, s=2)[:, :, ::-1, :]
                table = rope_s[:, t, kind:kind + 1, :].rearrange("p h (s d) -> p h s d", s=2)
                chain(nc.vector.tensor_tensor(rot_b[:, 0:w].rearrange("p (h s d) -> p h s d", h=n, s=2),
                                              swapped, table.to_broadcast([P, n, 2, HD // 2]), ALU.mult))
                if name[0] == "q":
                    nc.vector.tensor_tensor(rot[:, i % 2, 0:w], rot_a[:, 0:w], rot_b[:, 0:w],
                                            ALU.add).then_inc(rotated, 1)
                else:
                    chain(nc.vector.tensor_tensor(rot_a[:, 0:w], rot_a[:, 0:w], rot_b[:, 0:w], ALU.add))
                    dve.wait_ge(qk_rstd, i + 1)
                    nc.vector.tensor_tensor(rot[:, i % 2, 0:w].rearrange("p (h d) -> p h d", h=n),
                                            rot_a[:, 0:w].rearrange("p (h d) -> p h d", h=n),
                                            r_key[:, i % 2, 0:n].rearrange("p (h o) -> p h o", o=1).to_broadcast([P, n, HD]),
                                            ALU.mult).then_inc(rotated, 1)

            def silu(u):
                name, t = UNITS[u]
                e, half = STAGED.index(u), ["zA", "zB", "zC0", "zC1"].index(name) % 2
                dve.wait_ge(staged, e + 1)
                dve.wait_ge(turned, BATCH[0 if name in ("zA", "zB") else 2, t, 1] + 1)
                nc.vector.scalar_tensor_tensor(out=act_src[:, t, half * NCOL:(half + 1) * NCOL],
                                               in0=stage2[:, e % 2, :], scalar=1.0, in1=stage[:, e % 2, :],
                                               op0=ALU.add, op1=ALU.mult).then_inc(silu_done, 1)

            def gate(layer, t, half):
                heads = slice(half * CH, (half + 1) * CH)
                dve.wait_ge(head_copied, HC * layer + CH * (half + 1))
                dve.wait_ge(silu_done, ZU.index(UNIT[[["zA", "zB"], ["zC0", "zC1"]][layer][half], t]) + 1)
                g = act_src[:, t, half * NCOL:(half + 1) * NCOL].rearrange("p (h d) -> p h d", h=CH)
                nc.vector.tensor_tensor(g, g, y[:, t, heads, 0:HD], ALU.mult).then_inc(gated, 1)

            def mask(s):
                mixer, h = STEPS[s]
                c = s if s < HC else s - HC
                m = masks[:, "ABC".index(mixer), :]
                need = mixer if mixer != "C" else f"C{h // CH}"
                dve.wait_ge(scores_done, s + 1)
                dve.wait_ge(qk_rstd, SCORES_NEED[need] + 1)
                if s >= PROBS:
                    dve.wait_ge(probs_turned, s - PROBS + 1)
                first = BIG if mixer != "C" else neg_sinks[:, h:h + 1]
                for t, cols, mk in ((0, slice(0, P), m[:, P:2 * P]), (1, slice(P, 3 * P), m)):
                    last = nc.vector.tensor_tensor_reduce(out=probs[:, s % PROBS, cols], in0=sc[s % 2][:, cols], in1=mk,
                                                          scale=query_scale(mixer, h, t), scalar=first,
                                                          op0=ALU.add, op1=ALU.min, accum_out=neg_m[:, c, t:t + 1])
                last.then_inc(masked, 1)

            def count_probs(s):
                dve.wait_ge(probs_turned, s + 1)
                dve.wait_ge(masks_in, 48)
                if s >= 2:
                    dve.wait_ge(head_done, s - 1)
                nc.vector.tensor_tensor(probs_t[:, s % 2, :], tp[JOB["probs", s] % 2][:, 0:3 * P], count_t[:],
                                        ALU.mult).then_inc(probs_counted, 1)

            def copy_head(s):
                c = s if s < HC else s - HC
                o = ob[s % 2][:, 0:2 * VW].rearrange("p (t d) -> p t d", t=T)
                dve.wait_ge(head_done, s + 1)
                if s == 0:
                    dve.wait_ge(const_done, 8)
                if s >= HC:
                    dve.wait_ge(gated, 4)
                    dve.wait_ge(sink_done, c + 1)
                    chain(nc.vector.scalar_tensor_tensor(out=inv_l[:, c, :], in0=sink_e[:, c, :], scalar=2.0,
                                                         in1=o[:, :, HD], op0=ALU.mult, op1=ALU.add))
                    chain(nc.vector.reciprocal(inv_l[:, c, :], inv_l[:, c, :]))
                else:
                    chain(nc.vector.reciprocal(inv_l[:, c, :], o[:, :, HD]))
                nc.vector.tensor_tensor(y[:, :, c, 0:HD], o[:, :, 0:HD],
                                        inv_l[:, c, :].rearrange("p (t o) -> p t o", o=1).to_broadcast([P, T, HD]),
                                        ALU.mult).then_inc(head_copied, 1)

            def add_residual(u):
                name, t = UNITS[u]
                c = int(name[1]) * NCOL
                dve.wait_ge(proj_done, u + 1)
                if name[0] == "p":
                    dve.wait_ge(normed, 8)
                nc.vector.tensor_tensor(x_sb[:, t, c:c + NCOL], x_sb[:, t, c:c + NCOL], acc[u % 2][:],
                                        ALU.add).then_inc(out_added, 1)

            apply_gain(0, 0, 0)
            apply_gain(0, 0, 1)
            batch_lo(0)
            batch_lo(1)
            split_lo(0)
            apply_gain(0, 1, 0)
            split_lo(1)
            apply_gain(0, 1, 1)
            batch_lo(2)
            batch_lo(3)
            for p in (2, 3, 4):
                split_lo(p)
            dve.wait_ge(masks_in, 48)
            chain(nc.vector.tensor_scalar(neg_sinks[:], sinks[:], -1.0, None, ALU.mult))
            for n in range(N_SLOTS):
                if n in STEP_AT:
                    mask(STEP_AT[n])
                if n in PROBS_AT and PROBS_AT[n] < HA:
                    count_probs(PROBS_AT[n])
                if n in VALUE_AT:
                    copy_head(VALUE_AT[n])
                for layer, t, half in GATE_AT.get(n, []):
                    if not (n == END[UNIT["zC1", 1]] + 1 and t == 1):
                        gate(layer, t, half)
                for b in BATCH_AT.get(n, []):
                    if b >= 4:
                        batch_lo(b)
                for u in range(len(UNITS)):
                    if n == END[u] + 1:
                        if u in QK:
                            rotate(u)
                        elif u in ZU:
                            silu(u)
                        elif is_out(u):
                            add_residual(u)
                            if UNITS[u][0][0] == "o":
                                apply_gain(1, UNITS[u][1], int(UNITS[u][0][1]))
                if n == END[UNIT["zC1", 1]] + 1:
                    gate(1, 1, 1)
                for p in SPLIT_AT[n]:
                    split_lo(p)
            for u in OUTS:
                if END[u] + 1 >= N_SLOTS:
                    add_residual(u)


def packed_weights(even_in, even_out, odd_in, odd_out):
    heads = np.array([p // 2 + 8 * (p % 2) for p in range(HC)])
    cols = (heads[:, None] * HD + np.arange(HD)[None, :]).reshape(-1)
    width = HC * HD
    cut = {}
    for i, n in enumerate(("qA", "kA", "vA", "zA", "qB", "kB", "vB", "zB")):
        cut[n] = even_in[:, i * NCOL:(i + 1) * NCOL]
    q, kv, z = odd_in[:, 0:width][:, cols], odd_in[:, width:width + 256], odd_in[:, width + 256:][:, cols]
    out = odd_out[cols, :]
    cut["kvC"] = kv
    for i in range(2):
        half = slice(i * NCOL, (i + 1) * NCOL)
        cut[f"o{i}"], cut[f"qC{i}"], cut[f"zC{i}"], cut[f"p{i}"] = even_out[:, half], q[:, half], z[:, half], out[:, half]
    rows = []
    for name, w in CHUNKS:
        c = cut[name].reshape(K, P, w).transpose(1, 0, 2).reshape(P, -1, PER_DMA * PIECE)
        rows.append(c.transpose(1, 0, 2))
    return np.ascontiguousarray(np.concatenate(rows)), heads


def tables():
    inv = np.float32(ROPE_THETA) ** (-np.arange(0, HD, 2, dtype=np.float32) / np.float32(HD))
    ang = np.arange(S, dtype=np.float32)[:, None] * inv[None, :].astype(np.float32)
    cos, sin = np.cos(ang), np.sin(ang)
    i = np.arange(P)[:, None]
    dist = np.concatenate([P + i - np.arange(P)[None, :], i - np.arange(P)[None, :]], axis=1)
    count = sum(((dist >= 0) & (dist <= w) & (dist % d == 0)).astype(np.float32)
                for w, d in ((128, 1), (512, 4), (2048, 16)))
    keep = [count > 0, dist >= 0, (dist >= 0) & (dist < WINDOW)]
    prev, own = count[:, :P].T, count[:, P:].T
    m = np.concatenate([np.where(k, 0.0, NEG) for k in keep] + [own, prev, own], axis=1).astype(np.float32)
    return (np.concatenate([cos, cos], axis=1).astype(np.float32),
            np.concatenate([-sin, sin], axis=1).astype(np.float32), np.ascontiguousarray(m))


def kernel(**inputs):
    import concourse.bacc as bacc
    from concourse.bass_utils import run_bass_kernel_spmd as run

    a = {k: np.asarray(v) for k, v in inputs.items()}
    w, heads = packed_weights(a["w_in_even"][0], a["w_out_even"][0], a["w_in_odd"][0], a["w_out_odd"][0])
    g = [a[k][0] for k in ("qnorm_a", "knorm_a", "qnorm_b", "knorm_b", "qnorm_c", "knorm_c")]
    swapped = [np.concatenate([v[HD // 2:], v[:HD // 2]]) for v in g]
    cos, sin, masks = tables()
    arrays = {
        "x": a["x"][0],
        "w": w,
        "gains": np.concatenate([a["norm_even"][0], a["norm_odd"][0]])[None, :],
        "heads": np.concatenate(g + swapped)[None, :],
        "cos": cos,
        "sin": sin,
        "masks": masks,
        "sinks": a["sinks_c"][0][heads][None, :],
    }
    arrays = {k: np.ascontiguousarray(v) for k, v in arrays.items()}
    nc = bacc.Bacc("TRN2", target_bir_lowering=False, num_devices=1)
    args = [nc.dram_tensor(f"in_{k}", v.shape, mybir.dt.from_np(v.dtype), kind="ExternalInput").ap()
            for k, v in arrays.items()]
    out = nc.dram_tensor("out", (S, D), F32, kind="ExternalOutput").ap()
    bass_hybrid_dilated_moba_swa_sink_trunk(nc, *args, out)
    got = run(nc, [{f"in_{k}": v for k, v in arrays.items()}], core_ids=[0])
    return got.results[0]["out"].reshape(1, S, D)
```

```python
from contextlib import ExitStack

import numpy as np

import concourse.bass as bass
from concourse import mybir

F32 = mybir.dt.float32
F32R = mybir.dt.float32r
ALU = mybir.AluOpType
ACT = mybir.ActivationFunctionType
AX_X = mybir.AxisListType.X

P = 128
S = 256
T = S // P
D = 1024
K = D // P
HD = 64
HA = 8
HC = 16
NCOL = 512
CH = NCOL // HD
VW = HD + 1
EPS = 1e-6
NEG = -1e30
BIG = 3e38
ROPE_THETA = 10000.0
WINDOW = 128

CHUNKS = ([(n, NCOL) for n in ("qA", "kA", "vA", "qB", "kB", "vB", "zA", "zB", "o0", "o1")]
          + [("kvC", 256)] + [(n, NCOL) for n in ("qC0", "qC1", "zC0", "zC1", "p0", "p1")])
CHUNK = {n: i for i, (n, _) in enumerate(CHUNKS)}
PIECE = 1024
KPP = [PIECE // w for _, w in CHUNKS]
PIECES = [K // kpp for kpp in KPP]
FIRST_PIECE = [sum(PIECES[:i]) for i in range(len(CHUNKS))]
N_PIECES = sum(PIECES)
PER_DMA = 2
N_DMAS = N_PIECES // PER_DMA
RAW = 3
EARLY = 4
RING = 9

UNITS = [(c, t) for c in ("qA", "kA", "vA", "qB", "kB", "vB", "zA", "zB") for t in range(T)]
UNITS += [("o0", 0), ("o1", 0), ("o0", 1), ("o1", 1)]
UNITS += [("kvC", 0), ("qC0", 0), ("kvC", 1), ("qC0", 1), ("qC1", 0), ("qC1", 1)]
UNITS += [("zC0", 0), ("zC0", 1), ("zC1", 0), ("zC1", 1)]
UNITS += [("p0", 0), ("p1", 0), ("p0", 1), ("p1", 1)]
UNIT = {u: i for i, u in enumerate(UNITS)}


def is_out(u):
    return UNITS[u][0][0] in "op"


QK = [u for u, (c, _) in enumerate(UNITS) if c[0] in "qk"]
ZU = [u for u, (c, _) in enumerate(UNITS) if c[0] == "z"]
VU = [u for u, (c, _) in enumerate(UNITS) if c[0] == "v"]
STAGED = [u for u in range(len(UNITS)) if u in QK or u in ZU]
OUTS = [u for u in range(len(UNITS)) if is_out(u)]

LAST = len(UNITS) - 1

PARTS = {"q": 4, "k": 4, "v": 4, "z": 4, "o": 4, "p": 4, "kvC": 2}
SLOTS = []
for _u, (_c, _t) in enumerate(UNITS):
    _n = PARTS[_c] if _c in PARTS else PARTS[_c[0]]
    if _c in ("o0", "p0") and _t == 0:
        SLOTS += [(_u + j, i, _n) for i in range(_n) for j in range(2)]
    elif not (_c in ("o1", "p1") and _t == 0):
        SLOTS += [(_u, i, _n) for i in range(_n)]
N_SLOTS = len(SLOTS)
BEGIN = {u: min(n for n, s in enumerate(SLOTS) if s[0] == u) for u in range(len(UNITS))}
END = {u: max(n for n, s in enumerate(SLOTS) if s[0] == u) for u in range(len(UNITS))}


def end(chunk, t):
    return END[UNIT[chunk, t]]


STEPS = [("A", h) for h in range(HA)] + [("B", h) for h in range(HA)] + [("C", h) for h in range(HC)]
N_STEPS = len(STEPS)
SCORE_SLOTS = [
    22, 23, 27, 32, 36, 38, 39, 44, 46, 49, 51, 52, 53, 55, 58, 60, 97, 98, 99, 100, 101, 102, 103, 104,
    105, 106, 107, 108, 109, 110, 112, 113]
PROBS_SLOTS = [
    25, 27, 30, 34, 39, 42, 46, 47, 50, 52, 54, 55, 56, 58, 61, 62, 99, 100, 101, 102, 103, 104, 105, 106,
    107, 108, 109, 110, 111, 112, 114, 115]
VALUE_SLOTS = [
    28, 30, 32, 36, 42, 45, 48, 50, 52, 53, 56, 57, 58, 61, 62, 64, 100, 101, 102, 103, 104, 105, 106,
    107, 108, 109, 110, 111, 112, 113, 115, 116]
STEP_AT = {n: s for s, n in enumerate(SCORE_SLOTS)}
PROBS_AT = {n: s for s, n in enumerate(PROBS_SLOTS)}
VALUE_AT = {n: s for s, n in enumerate(VALUE_SLOTS)}
assert len(STEP_AT) == len(PROBS_AT) == len(VALUE_AT) == N_STEPS
PROBS = 3

TURN_SLOTS = [9, 14, 19, 21, 34, 36, 42, 45, 90, 90, 95, 95, 98, 104]
TURN_AT = {}
for _i, _n in enumerate(TURN_SLOTS):
    TURN_AT.setdefault(_n, []).append(_i)

BATCHES = [(phase, t, half) for phase in range(4) for t in range(T) for half in range(2)]
BATCH = {b: i for i, b in enumerate(BATCHES)}
FIRST_TURNED = BATCH[1, 0, 0]
BATCH_SLOTS = [0, 0, 2, 3, 60, 67, 67, 71, 73, 77, 81, 84, 113, 118, 119, 122]
GATE_KEYS = [(layer, t, half) for layer in range(2) for t in range(T) for half in range(2)]
GATE_SLOTS = [58, 64, 63, 69, 110, 116, 110, 120]
SUMSQ0_AT = 2
SUMSQ1_AT = 7
BATCH_AT = {}
for _b, _n in enumerate(BATCH_SLOTS):
    BATCH_AT.setdefault(_n, []).append(_b)


def gate_after_silu(g):
    layer, t, half = g
    u = UNIT[[["zA", "zB"], ["zC0", "zC1"]][layer][half], t]
    return GATE_SLOTS[GATE_KEYS.index(g)] == END[u] + 1


GATES = sorted(GATE_KEYS, key=lambda g: (GATE_SLOTS[GATE_KEYS.index(g)], gate_after_silu(g)))
GATE_AT = {}
for _g in GATES:
    GATE_AT.setdefault(GATE_SLOTS[GATE_KEYS.index(_g)], []).append(_g)

JOBS = []
for _n in range(N_SLOTS):
    JOBS += [("turn", i) for i in TURN_AT.get(_n, [])]
    JOBS += [("probs", PROBS_AT[_n])] if _n in PROBS_AT else []
    JOBS += [("batch", b) for b in BATCH_AT.get(_n, []) if b >= FIRST_TURNED]
JOB = {j: i for i, j in enumerate(JOBS)}


def last_use(piece):
    c = max(i for i in range(len(CHUNKS)) if FIRST_PIECE[i] <= piece)
    return max(UNIT[CHUNKS[c][0], t] for t in range(T))


SPLIT_SLOTS = [
    -1, -1, -1, -1, 4, 6, 6, 7, 8, 8, 8, 12, 17, 18, 21, 24, 26, 26, 29, 29, 32, 33, 34, 35, 41, 41, 44,
    45, 49, 50, 51, 53, 57, 58, 59, 59, 63, 65, 65, 65, 68, 76, 76, 79, 79, 80, 83, 83, 89, 89, 93, 93,
    93, 95, 96, 102, 102, 105, 106, 109, 111, 111, 114, 116, 116, 119]
ACT_SPLIT_FIRST = [4, 17, 29, 44, 50, 51, 53, 58, 59, 65, 76, 80, 83, 89, 105]
DVE_SPLIT_FIRST = [4, 6, 26, 34, 41, 45, 51, 59, 68, 89, 114]
ACT_EXP_FIRST = [104]
DVE_UNIT_FIRST = [44, 71]
SPLIT_AT = {n: [p for p in range(N_PIECES) if SPLIT_SLOTS[p] == n] for n in range(-1, N_SLOTS)}


def hybrid_trunk(nc, x_d, xt_d, w_d, gains_d, heads_d, cos_d, sin_d, masks_d, sinks_d, out_d):
    with ExitStack() as ctx:
        def sb(name, shape, dt=F32):
            return ctx.enter_context(nc.sbuf_tensor(name, shape, dt))

        def pb(name):
            return ctx.enter_context(nc.psum_tensor(name, [P, 512], F32))

        def sem(name):
            return ctx.enter_context(nc.semaphore(name))

        x_sb = sb("x_sb", [P, T, D])
        gains = sb("gains", [P, 2, K])
        head_row = sb("head_row", [1, 12 * HD])
        head_g = sb("head_g", [P, 2, 6, HD])
        cos_sb = sb("cos_sb", [P, T, HD])
        sin_sb = sb("sin_sb", [P, T, HD])
        rope_c = sb("rope_c", [P, T, 6, HD])
        rope_s = sb("rope_s", [P, T, 6, HD])
        masks = sb("masks", [P, 3, 2 * P])
        count_t = sb("count_t", [P, 3 * P])
        sinks = sb("sinks", [P, HC])
        neg_sinks = sb("neg_sinks", [P, HC])
        ident = sb("ident", [P, P])
        minus_half = sb("minus_half", [P, CH])
        raw = sb("raw", [P, RAW, PER_DMA, PIECE])
        w_hi = sb("w_hi", [P, RING, PIECE], F32R)
        w_lo = sb("w_lo", [P, RING, PIECE], F32R)
        a_hi = sb("a_hi", [P, K, S], F32R)
        a_lo = sb("a_lo", [P, K, S], F32R)
        act_src = sb("act_src", [P, T, D])
        stage = sb("stage", [P, 2, NCOL])
        stage2 = sb("stage2", [P, 2, NCOL])
        rot_a = sb("rot_a", [P, NCOL])
        rot_b = sb("rot_b", [P, NCOL])
        rot = sb("rot", [P, 2, NCOL])
        msq = sb("msq", [P, 2, CH])
        r_tmp = sb("r_tmp", [P, 2, CH])
        r_key = sb("r_key", [P, 2, CH])
        r_qry = sb("r_qry", [P, 8, CH])
        qk_t = sb("qk_t", [P, 16, S])
        kc_t = sb("kc_t", [P, S])
        va = sb("va", [P, T, HA, VW])
        vb = sb("vb", [P, T, HA, VW])
        vc = sb("vc", [P, T, 2, VW])
        probs = sb("probs", [P, PROBS, 3 * P])
        probs_t = sb("probs_t", [P, 2, 3 * P])
        neg_m = sb("neg_m", [P, HC, T])
        y = sb("y", [P, T, HC, VW])
        inv_l = sb("inv_l", [P, HC, T])
        sink_e = sb("sink_e", [P, HC, T])
        ssq = sb("ssq", [P, 4, 2])
        ms = sb("ms", [P, 4])
        rstd = sb("rstd", [P, 4])
        half_rstd = sb("half_rstd", [P, 4])

        acc = [pb(f"acc{i}") for i in range(2)]
        sc = [pb(f"sc{i}") for i in range(2)]
        tp = [pb(f"tp{i}") for i in range(2)]
        ob = [pb(f"ob{i}") for i in range(2)]

        x_in = [sem(f"x_in{t}") for t in range(T)]
        xt_in = [sem(f"xt_in{i}") for i in range(2 * T)]
        gain_in = sem("gain_in")
        heads_in = sem("heads_in")
        tables_in = sem("tables_in")
        masks_in = sem("masks_in")
        early_in = [sem(f"early_in{i}") for i in range(EARLY)]
        raw_in = [sem(f"raw_in{i}") for i in range(RAW)]
        hi_done = sem("hi_done")
        lo_done = sem("lo_done")
        const_done = sem("const_done")
        gp_chain = sem("gp_chain")
        dve_chain = sem("dve_chain")
        sumsq_done = sem("sumsq_done")
        rstd_done = sem("rstd_done")
        turned = sem("turned")
        a_hi_done = sem("a_hi_done")
        a_lo_done = sem("a_lo_done")
        proj_done = sem("proj_done")
        out_added = sem("out_added")
        staged = sem("staged")
        msq_done = sem("msq_done")
        qk_rstd = sem("qk_rstd")
        cos_done = sem("cos_done")
        rotated = sem("rotated")
        silu_done = sem("silu_done")
        qk_turned = sem("qk_turned")
        qk_ready = sem("qk_ready")
        v_ready = sem("v_ready")
        scores_done = sem("scores_done")
        masked = sem("masked")
        exp_done = sem("exp_done")
        probs_turned = sem("probs_turned")
        probs_counted = sem("probs_counted")
        probs_copied = sem("probs_copied")
        head_done = sem("head_done")
        head_copied = sem("head_copied")
        sink_done = sem("sink_done")
        gated = sem("gated")
        stored = sem("stored")

        block = ctx.enter_context(nc.Block())

        def parts_of(name):
            c = CHUNK[name]
            return CHUNKS[c][1], KPP[c], FIRST_PIECE[c]

        def probs_in_sbuf(eng, s):
            if s < HA:
                eng.wait_ge(probs_counted, s + 1)
            else:
                eng.wait_ge(probs_copied, s - HA + 1)

        def bank_free(eng, j):
            if j >= 2:
                kind, i = JOBS[j - 2]
                if kind == "turn":
                    eng.wait_ge(qk_ready, i + 1)
                elif kind == "probs":
                    probs_in_sbuf(eng, i)
                else:
                    eng.wait_ge(a_lo_done, 4 * (i + 1))

        def query_scale(mixer, h, t):
            col = {"A": 0, "B": 2, "C": 4 + 2 * (h // CH)}[mixer] + t
            return r_qry[:, col, h % CH:h % CH + 1]

        def q_of(mixer, h):
            side = HD * (h % 2)
            return qk_t[side:side + HD, {"A": 0, "B": 8, "C": 0}[mixer] + h // 2, :]

        def k_of(mixer, h):
            side = HD * (h % 2)
            if mixer == "C":
                return kc_t[side:side + HD, :]
            return qk_t[side:side + HD, {"A": 4, "B": 12}[mixer] + h // 2, :]

        def v_of(mixer, h, t):
            if mixer == "C":
                return vc[:, t, h % 2, :]
            return (va if mixer == "A" else vb)[:, t, h, :]

        SCORES_NEED = {"A": QK.index(UNIT["kA", 1]), "B": QK.index(UNIT["kB", 1]),
                       "C0": QK.index(UNIT["qC0", 1]), "C1": QK.index(UNIT["qC1", 1])}

        @block.sync
        def _(sp):
            def load_piece(d, half):
                if d >= RAW:
                    sp.wait_ge(lo_done, PER_DMA * (d - RAW) + half + 1)
                sp.dma_start(raw[:, d % RAW, half, :], w_d[d, :, half * PIECE:(half + 1) * PIECE]
                             ).then_inc(early_in[d] if half == 0 else raw_in[d % RAW], 16)

            sp.dma_start(act_src[:, 0, 0:NCOL], xt_d[0, :, :]).then_inc(xt_in[0], 16)
            sp.dma_start(gains[:], gains_d.rearrange("p (l k) -> p l k", l=2)).then_inc(gain_in, 16)
            sp.dma_start(act_src[:, 0, NCOL:D], xt_d[1, :, :]).then_inc(xt_in[1], 16)
            for d in range(2):
                load_piece(d, 0)
                load_piece(d, 1)
            sp.dma_start(act_src[:, 1, 0:NCOL], xt_d[2, :, :]).then_inc(xt_in[2], 16)
            sp.dma_start(act_src[:, 1, NCOL:D], xt_d[3, :, :]).then_inc(xt_in[3], 16)
            sp.dma_start(x_sb[:, 0, :], x_d[0:P, :]).then_inc(x_in[0], 16)
            sp.dma_start(head_row[:], heads_d).then_inc(heads_in, 16)
            sp.dma_start(cos_sb[:], cos_d.rearrange("(t p) n -> p t n", p=P)).then_inc(tables_in, 16)
            sp.dma_start(sin_sb[:], sin_d.rearrange("(t p) n -> p t n", p=P)).then_inc(tables_in, 16)
            load_piece(2, 0)
            load_piece(2, 1)
            load_piece(3, 0)
            sp.dma_start(x_sb[:, 1, :], x_d[P:S, :]).then_inc(x_in[1], 16)
            load_piece(3, 1)
            for d in range(EARLY, N_DMAS):
                if d >= RAW:
                    sp.wait_ge(lo_done, PER_DMA * (d - RAW + 1))
                sp.dma_start(raw[:, d % RAW, :, :].rearrange("p a n -> p (a n)"),
                             w_d[d, :, :]).then_inc(raw_in[d % RAW], 16)
                if d == 8:
                    sp.dma_start(masks[:], masks_d[:, 0:6 * P].rearrange("p (m n) -> p m n", m=3)
                                 ).then_inc(masks_in, 16)
                    sp.dma_start(count_t[:], masks_d[:, 6 * P:9 * P]).then_inc(masks_in, 16)
                    sp.dma_start(sinks[:], sinks_d.to_broadcast([P, HC])).then_inc(masks_in, 16)
            stores = [(u, int(UNITS[u][0][1]) * NCOL, NCOL) for u in OUTS[4:7]]
            stores += [(LAST, NCOL + side * NCOL // 2, NCOL // 2) for side in range(2)]
            for i, (u, c, width) in enumerate(stores):
                t = UNITS[u][1]
                sp.wait_ge(out_added, 4 + i + 1)
                sp.dma_start(out_d[t * P:(t + 1) * P, c:c + width], x_sb[:, t, c:c + width]).then_inc(stored, 16)
            sp.wait_ge(stored, 16 * len(stores))

        @block.gpsimd
        def _(pool):
            steps = [0]

            def chain(ins):
                steps[0] += 1
                ins.then_inc(gp_chain, 1)
                pool.wait_ge(gp_chain, steps[0])

            chain(nc.gpsimd.memset(minus_half[:], -0.5))
            chain(nc.gpsimd.memset(ident[:], 0.0))
            nc.gpsimd.affine_select(out=ident[:], in_=ident[:], compare_op=ALU.not_equal, fill=1.0, base=0,
                                    pattern=[[-1, P]], channel_multiplier=1).then_inc(const_done, 1)
            for v in (va, vb, vc):
                nc.gpsimd.memset(v[:, :, :, HD:VW], 2.0).then_inc(const_done, 1)

            def row_norm(i):
                pool.wait_ge(sumsq_done, 2 * (i + 1))
                chain(nc.gpsimd.tensor_tensor(ms[:, i:i + 1], ssq[:, i, 0:1], ssq[:, i, 1:2], ALU.add))
                chain(nc.gpsimd.tensor_scalar(ms[:, i:i + 1], ms[:, i:i + 1], 1.0 / D, EPS, ALU.mult, ALU.add))
                chain(nc.gpsimd.tensor_tensor(rstd[:, i:i + 1], ms[:, i:i + 1], minus_half[:, 0:1], ALU.pow))
                nc.gpsimd.tensor_scalar(half_rstd[:, i:i + 1], rstd[:, i:i + 1], 0.5, None,
                                        ALU.mult).then_inc(rstd_done, 1)

            def rotate_cos(i):
                u = QK[i]
                name, t = UNITS[u]
                e = STAGED.index(u)
                kind = {"qA": 0, "qB": 2, "qC0": 4, "qC1": 4}[name]
                pool.wait_ge(staged, e + 1)
                pool.wait_ge(const_done, 6 + 2 * t)
                if i >= 1:
                    pool.wait_ge(rotated, i)
                nc.gpsimd.tensor_tensor(rot_a[:].rearrange("p (h d) -> p h d", h=CH),
                                        stage[:, e % 2, :].rearrange("p (h d) -> p h d", h=CH),
                                        rope_c[:, t, kind:kind + 1, :].to_broadcast([P, CH, HD]),
                                        ALU.mult).then_inc(cos_done, 1)

            def head_norm(i):
                u = QK[i]
                name, t = UNITS[u]
                n = 2 if name == "kvC" else CH
                pool.wait_ge(msq_done, i + 1)
                if i >= 2:
                    pool.wait_ge(rotated, i - 1)
                    pool.wait_ge(qk_rstd, i - 1)
                chain(nc.gpsimd.tensor_scalar(r_tmp[:, i % 2, 0:n], msq[:, i % 2, 0:n], 1.0 / HD, EPS,
                                              ALU.mult, ALU.add))
                if name[0] == "k":
                    nc.gpsimd.tensor_tensor(r_key[:, i % 2, 0:n], r_tmp[:, i % 2, 0:n], minus_half[:, 0:n],
                                            ALU.pow).then_inc(qk_rstd, 1)
                else:
                    col = {"qA": 0, "qB": 2, "qC0": 4, "qC1": 6}[name] + t
                    chain(nc.gpsimd.tensor_tensor(r_qry[:, col, :], r_tmp[:, i % 2, :], minus_half[:], ALU.pow))
                    nc.gpsimd.tensor_scalar(r_qry[:, col, :], r_qry[:, col, :], -float(HD) ** -0.5, None,
                                            ALU.mult).then_inc(qk_rstd, 1)

            def rope_tables(t):
                for dst, src, g in ((rope_c, cos_sb, 0), (rope_s, sin_sb, 1)):
                    nc.gpsimd.tensor_tensor(dst[:, t, :, :], head_g[:, g, :, :],
                                            src[:, t:t + 1, :].to_broadcast([P, 6, HD]),
                                            ALU.mult).then_inc(const_done, 1)

            pool.wait_ge(heads_in, 16)
            chain(nc.gpsimd.partition_broadcast(head_g[:].rearrange("p a b n -> p (a b n)"), head_row[:], P))
            row_norm(0)
            pool.wait_ge(tables_in, 32)
            rope_tables(0)
            qk_end = {}
            for i, u in enumerate(QK):
                qk_end.setdefault(END[u] + 1, []).append(i)
            for n in range(N_SLOTS):
                for i in qk_end.get(n, []):
                    if UNITS[QK[i]][0][0] == "q":
                        rotate_cos(i)
                    head_norm(i)
                    if i == 0:
                        row_norm(1)
                        rope_tables(1)
                if n == BEGIN[UNIT["vB", 0]]:
                    pool.wait_ge(masks_in, 48)
                    nc.gpsimd.tensor_scalar(neg_sinks[:], sinks[:], -1.0, None, ALU.mult).then_inc(const_done, 1)
                for t in range(T):
                    if n == END[UNIT["o1", t]] + 1:
                        row_norm(2 + t)

        @block.scalar
        def _(act):
            def sum_squares(i, half):
                t = i % 2
                if i < 2:
                    act.wait_ge(x_in[t], 16)
                n = 2 * i + half
                if n >= 1:
                    act.wait_ge(sumsq_done, n)
                if i >= 2:
                    act.wait_ge(head_copied, HC)
                nc.scalar.activation(ob[0][:], x_sb[:, t, half * NCOL:(half + 1) * NCOL], ACT.Square,
                                     accum_out=ssq[:, i, half:half + 1]).then_inc(sumsq_done, 1)

            def split_hi(p):
                d = p // PER_DMA
                if p in range(0, PER_DMA * EARLY, PER_DMA):
                    act.wait_ge(early_in[d], 16)
                else:
                    act.wait_ge(raw_in[d % RAW], 16 * (d // RAW + 1))
                if p >= RING:
                    act.wait_ge(proj_done, last_use(p - RING) + 1)
                nc.scalar.activation(w_hi[:, p % RING, :], raw[:, d % RAW, p % PER_DMA, :],
                                     ACT.Copy).then_inc(hi_done, 1)

            def batch_hi(b):
                phase, t, half = BATCHES[b]
                if phase > 0:
                    act.wait_ge(turned, b - FIRST_TURNED + 1)
                    before = {1: UNIT["zB", t], 2: UNIT["o1", t], 3: UNIT["zC1", t]}[phase]
                    act.wait_ge(proj_done, before + 1)
                cols = slice(t * P, (t + 1) * P)
                if phase == 0:
                    src = act_src[:, t, half * NCOL:(half + 1) * NCOL]
                else:
                    src = tp[JOB["batch", b] % 2][:]
                if phase in (0, 2):
                    if b == 0:
                        act.wait_ge(gain_in, 16)
                    if phase == 0:
                        act.wait_ge(xt_in[b], 16)
                    for j in range(4):
                        k = 4 * half + j
                        nc.scalar.activation(a_hi[:, k, cols], src[:, j * P:(j + 1) * P], ACT.Copy,
                                             scale=gains[:, phase // 2, k:k + 1]).then_inc(a_hi_done, 1)
                else:
                    nc.scalar.activation(a_hi[:, 4 * half:4 * half + 4, cols],
                                         src.rearrange("p (k n) -> p k n", k=4),
                                         ACT.Copy).then_inc(a_hi_done, 4)

            def read_unit(u):
                name, t = UNITS[u]
                act.wait_ge(proj_done, u + 1)
                bank = acc[u % 2]
                row = 2 * int(u > UNIT["o1", 1]) + t
                act.wait_ge(rstd_done, row + 1)
                scale, half_scale = rstd[:, row:row + 1], half_rstd[:, row:row + 1]
                if u in STAGED:
                    e = STAGED.index(u)
                    if e >= 2:
                        former = STAGED[e - 2]
                        if former in QK:
                            act.wait_ge(rotated, QK.index(former) + 1)
                        else:
                            act.wait_ge(silu_done, ZU.index(former) + 1)
                    width = 2 * HD if name == "kvC" else NCOL
                    nc.scalar.activation(stage[:, e % 2, 0:width], bank[:, 0:width], ACT.Copy, scale=scale)
                    if name == "kvC":
                        nc.scalar.activation(vc[:, t, :, 0:HD],
                                             bank[:, width:2 * width].rearrange("p (h d) -> p h d", h=2),
                                             ACT.Copy, scale=scale).then_inc(v_ready, 1)
                    fn, scale = (ACT.Tanh, half_scale) if name[0] == "z" else (ACT.Square, scale)
                    nc.scalar.activation(stage2[:, e % 2, 0:width], bank[:, 0:width], fn,
                                         scale=scale).then_inc(staged, 1)
                else:
                    v = va if name == "vA" else vb
                    nc.scalar.activation(v[:, t, :, 0:HD], bank[:].rearrange("p (h d) -> p h d", h=HA),
                                         ACT.Copy, scale=scale).then_inc(v_ready, 1)

            def copy_turned(i):
                name, t = UNITS[QK[i]]
                act.wait_ge(qk_turned, i + 1)
                cols = slice(t * P, (t + 1) * P)
                bank = tp[JOB["turn", i] % 2]
                if name == "kvC":
                    nc.scalar.activation(kc_t[:, cols], bank[:, 0:P], ACT.Copy).then_inc(qk_ready, 1)
                else:
                    at = {"qA": 0, "kA": 4, "qB": 8, "kB": 12, "qC0": 0, "qC1": 4}[name]
                    if name[1] == "C":
                        act.wait_ge(scores_done, HA)
                    nc.scalar.activation(qk_t[:, at:at + 4, cols], bank[:].rearrange("p (k n) -> p k n", k=4),
                                         ACT.Copy).then_inc(qk_ready, 1)

            def softmax_exp(s):
                act.wait_ge(masked, s + 1)
                c = s if s < HC else s - HC
                for t, cols in ((0, slice(0, P)), (1, slice(P, 3 * P))):
                    last = nc.scalar.activation(probs[:, s % PROBS, cols], probs[:, s % PROBS, cols], ACT.Exp,
                                                bias=neg_m[:, c, t:t + 1], scale=-1.0)
                last.then_inc(exp_done, 1)
                if s >= HC:
                    nc.scalar.activation(sink_e[:, c, :], neg_m[:, c, :], ACT.Exp,
                                         bias=sinks[:, c:c + 1]).then_inc(sink_done, 1)

            def copy_probs(s):
                act.wait_ge(probs_turned, s + 1)
                if s >= 2:
                    act.wait_ge(head_done, s - 1)
                nc.scalar.activation(probs_t[:, s % 2, :], tp[JOB["probs", s] % 2][:, 0:3 * P],
                                     ACT.Copy).then_inc(probs_copied, 1)

            assert SPLIT_AT[-1] == [0, 1, 2, 3]
            act.wait_ge(gp_chain, 1)
            nc.scalar.activation(half_rstd[:, 0:1], minus_half[:, 0:1], ACT.Copy)
            batch_hi(0)
            batch_hi(1)
            split_hi(0)
            split_hi(1)
            split_hi(2)
            split_hi(3)
            for n in range(N_SLOTS):
                if n in ACT_SPLIT_FIRST:
                    for p in SPLIT_AT[n]:
                        split_hi(p)
                for i in TURN_AT.get(n, []):
                    copy_turned(i)
                if n in PROBS_AT and PROBS_AT[n] >= HA:
                    copy_probs(PROBS_AT[n])
                for b in BATCH_AT.get(n, []):
                    if b >= 2:
                        batch_hi(b)
                if n in STEP_AT and n in ACT_EXP_FIRST:
                    softmax_exp(STEP_AT[n])
                for u in range(len(UNITS)):
                    if n == END[u] + 1 and not is_out(u):
                        read_unit(u)
                if n in STEP_AT and n not in ACT_EXP_FIRST:
                    softmax_exp(STEP_AT[n])
                if n == SUMSQ0_AT:
                    sum_squares(0, 0)
                    sum_squares(0, 1)
                if n == SUMSQ1_AT:
                    sum_squares(1, 0)
                    sum_squares(1, 1)
                for t in range(T):
                    for half in range(2):
                        if n == end(f"o{half}", t) + 1:
                            act.wait_ge(out_added, 2 * t + half + 1)
                            sum_squares(2 + t, half)
                if n not in ACT_SPLIT_FIRST:
                    for p in SPLIT_AT[n]:
                        split_hi(p)

        @block.tensor
        def _(pe):
            def project(n):
                u, part, parts = SLOTS[n]
                name, t = UNITS[u]
                width, kpp, first = parts_of(name)
                bank = acc[u % 2][:, 0:width]
                phase = 0 if u < UNIT["o0", 0] else 1 if u < UNIT["kvC", 0] else 2 if u < UNIT["p0", 0] else 3
                if u == LAST and part == parts // 2:
                    pe.wait_ge(out_added, OUTS.index(u - 1) + 1)
                if part == 0:
                    if u >= 2:
                        if is_out(u - 2):
                            pe.wait_ge(out_added, OUTS.index(u - 2) + 1)
                        elif u - 2 in STAGED:
                            pe.wait_ge(staged, STAGED.index(u - 2) + 1)
                        else:
                            pe.wait_ge(v_ready, VU.index(u - 2) + 1)
                tiles, cut = range(K * part // parts, K * (part + 1) // parts), slice(0, width)
                if u == LAST:
                    side = 2 * part // parts
                    tiles = range(K * (2 * part % parts) // parts, K * (2 * part % parts + 2) // parts)
                    cut = slice(side * NCOL // 2, (side + 1) * NCOL // 2)
                    bank = acc[(u + side) % 2][:, cut]
                for k in tiles:
                    p = first + k // kpp
                    if k % 4 == 0 or phase in (0, 2):
                        pe.wait_ge(a_lo_done, 4 * BATCH[phase, t, k // 4] + (k % 4 + 1 if phase in (0, 2) else 4))
                    if k % kpp == 0 or k == tiles[0]:
                        pe.wait_ge(lo_done, p + 1)
                    cols = slice((k % kpp) * width + cut.start, (k % kpp) * width + cut.stop)
                    hi, lo = w_hi[:, p % RING, cols], w_lo[:, p % RING, cols]
                    ah, al = a_hi[:, k, t * P:(t + 1) * P], a_lo[:, k, t * P:(t + 1) * P]
                    nc.tensor.matmul(bank, ah, hi, start=(k == 0), stop=False)
                    nc.tensor.matmul(bank, ah, lo, start=False, stop=False)
                    last = nc.tensor.matmul(bank, al, hi, start=False, stop=(k == K - 1))
                if part == parts - 1 or u == LAST and part == parts // 2 - 1:
                    last.then_inc(proj_done, 1)

            def scores(s):
                mixer, h = STEPS[s]
                need = mixer if mixer != "C" else f"C{h // CH}"
                pe.wait_ge(qk_ready, SCORES_NEED[need] + 1)
                if s >= 2:
                    pe.wait_ge(masked, s - 1)
                q, k = q_of(mixer, h), k_of(mixer, h)
                nc.tensor.matmul(sc[s % 2][:, 0:P], q[:, 0:P], k[:, 0:P], start=True, stop=True)
                nc.tensor.matmul(sc[s % 2][:, P:3 * P], q[:, P:2 * P], k[:, 0:2 * P],
                                 start=True, stop=True).then_inc(scores_done, 1)

            def turn_probs(s):
                pe.wait_ge(exp_done, s + 1)
                bank_free(pe, JOB["probs", s])
                for i in range(3):
                    last = nc.tensor.transpose(tp[JOB["probs", s] % 2][:, i * P:(i + 1) * P],
                                               probs[:, s % PROBS, i * P:(i + 1) * P], ident[:])
                last.then_inc(probs_turned, 1)

            def values(s):
                mixer, h = STEPS[s]
                probs_in_sbuf(pe, s)
                pe.wait_ge(v_ready, {"A": 2, "B": 4, "C": 6}[mixer])
                if s >= 2:
                    pe.wait_ge(head_copied, s - 1)
                if s in (0, HC):
                    pe.wait_ge(sumsq_done, 4 if s == 0 else 8)
                pt, o = probs_t[:, s % 2, :], ob[s % 2]
                nc.tensor.matmul(o[:, 0:VW], pt[:, 0:P], v_of(mixer, h, 0), start=True, stop=True)
                nc.tensor.matmul(o[:, VW:2 * VW], pt[:, P:2 * P], v_of(mixer, h, 0), start=True, stop=False)
                nc.tensor.matmul(o[:, VW:2 * VW], pt[:, 2 * P:3 * P], v_of(mixer, h, 1),
                                 start=False, stop=True).then_inc(head_done, 1)

            def turn_qk(i):
                pe.wait_ge(rotated, i + 1)
                bank_free(pe, JOB["turn", i])
                for j in range(1 if UNITS[QK[i]][0] == "kvC" else 4):
                    last = nc.tensor.transpose(tp[JOB["turn", i] % 2][:, j * P:(j + 1) * P],
                                               rot[:, i % 2, j * P:(j + 1) * P], ident[:])
                last.then_inc(qk_turned, 1)

            def turn_batch(b):
                phase, t, half = BATCHES[b]
                src = x_sb if phase == 2 else act_src
                if phase == 2:
                    pe.wait_ge(out_added, 2 * t + half + 1)
                else:
                    pe.wait_ge(gated, GATES.index((phase // 2, t, half)) + 1)
                bank_free(pe, JOB["batch", b])
                for j in range(4):
                    c = half * NCOL + j * P
                    last = nc.tensor.transpose(tp[JOB["batch", b] % 2][:, j * P:(j + 1) * P],
                                               src[:, t, c:c + P], ident[:])
                last.then_inc(turned, 1)

            def keep_busy(n):
                for _ in range(n):
                    nc.tensor.matmul(acc[1][:, 0:P], ident[:], ident[:], start=True, stop=True)

            pe.wait_ge(const_done, 4)
            keep_busy(14)
            for n in range(N_SLOTS):
                for i in TURN_AT.get(n, []):
                    turn_qk(i)
                if n in PROBS_AT:
                    turn_probs(PROBS_AT[n])
                if n in STEP_AT:
                    scores(STEP_AT[n])
                for b in BATCH_AT.get(n, []):
                    if b >= FIRST_TURNED:
                        turn_batch(b)
                if n in VALUE_AT:
                    values(VALUE_AT[n])
                project(n)

        @block.vector
        def _(dve):
            steps = [0]

            def chain(ins):
                steps[0] += 1
                ins.then_inc(dve_chain, 1)
                dve.wait_ge(dve_chain, steps[0])

            def split_lo(p):
                dve.wait_ge(hi_done, p + 1)
                nc.vector.tensor_tensor(w_lo[:, p % RING, :], raw[:, p // PER_DMA % RAW, p % PER_DMA, :],
                                        w_hi[:, p % RING, :].bitcast(F32), ALU.subtract).then_inc(lo_done, 1)

            def batch_lo(b):
                phase, t, half = BATCHES[b]
                cols = slice(t * P, (t + 1) * P)
                if phase == 0:
                    src = act_src[:, t, half * NCOL:(half + 1) * NCOL]
                else:
                    src = tp[JOB["batch", b] % 2][:]
                if phase > 0:
                    dve.wait_ge(a_hi_done, 4 * (b + 1))
                if phase in (0, 2):
                    if b == 0:
                        dve.wait_ge(gain_in, 16)
                    for j in range(4):
                        k = 4 * half + j
                        if phase == 0:
                            dve.wait_ge(a_hi_done, 4 * b + j + 1)
                        nc.vector.scalar_tensor_tensor(out=a_lo[:, k, cols], in0=src[:, j * P:(j + 1) * P],
                                                       scalar=gains[:, phase // 2, k:k + 1],
                                                       in1=a_hi[:, k, cols].bitcast(F32),
                                                       op0=ALU.mult, op1=ALU.subtract).then_inc(a_lo_done, 1)
                else:
                    ks = slice(4 * half, 4 * half + 4)
                    nc.vector.tensor_tensor(a_lo[:, ks, cols], src.rearrange("p (k n) -> p k n", k=4),
                                            a_hi[:, ks, cols].bitcast(F32), ALU.subtract).then_inc(a_lo_done, 4)

            def rotate(u):
                name, t = UNITS[u]
                i, e = QK.index(u), STAGED.index(u)
                n = 2 if name == "kvC" else CH
                kind = {"qA": 0, "kA": 1, "qB": 2, "kB": 3, "qC0": 4, "qC1": 4, "kvC": 5}[name]
                w = n * HD
                dve.wait_ge(staged, e + 1)
                if i >= 2:
                    dve.wait_ge(qk_rstd, i - 1)
                    dve.wait_ge(qk_turned, i - 1)
                if i < 2:
                    dve.wait_ge(const_done, 6 + 2 * i)
                nc.vector.tensor_reduce(msq[:, i % 2, 0:n],
                                        stage2[:, e % 2, 0:w].rearrange("p (h d) -> p h d", h=n),
                                        AX_X, ALU.add).then_inc(msq_done, 1)
                if i >= 1:
                    dve.wait_ge(rotated, i)
                src = stage[:, e % 2, 0:w]
                if name[0] == "k":
                    nc.vector.tensor_tensor(rot_a[:, 0:w].rearrange("p (h d) -> p h d", h=n),
                                            src.rearrange("p (h d) -> p h d", h=n),
                                            rope_c[:, t, kind:kind + 1, :].to_broadcast([P, n, HD]), ALU.mult)
                swapped = src.rearrange("p (h s d) -> p h s d", h=n, s=2)[:, :, ::-1, :]
                table = rope_s[:, t, kind:kind + 1, :].rearrange("p h (s d) -> p h s d", s=2)
                chain(nc.vector.tensor_tensor(rot_b[:, 0:w].rearrange("p (h s d) -> p h s d", h=n, s=2),
                                              swapped, table.to_broadcast([P, n, 2, HD // 2]), ALU.mult))
                if name[0] == "q":
                    dve.wait_ge(cos_done, 1 + [j for j in range(len(QK)) if UNITS[QK[j]][0][0] == "q"].index(i))
                    nc.vector.tensor_tensor(rot[:, i % 2, 0:w], rot_a[:, 0:w], rot_b[:, 0:w],
                                            ALU.add).then_inc(rotated, 1)
                else:
                    chain(nc.vector.tensor_tensor(rot_a[:, 0:w], rot_a[:, 0:w], rot_b[:, 0:w], ALU.add))
                    dve.wait_ge(qk_rstd, i + 1)
                    nc.vector.tensor_tensor(rot[:, i % 2, 0:w].rearrange("p (h d) -> p h d", h=n),
                                            rot_a[:, 0:w].rearrange("p (h d) -> p h d", h=n),
                                            r_key[:, i % 2, 0:n].rearrange("p (h o) -> p h o", o=1).to_broadcast([P, n, HD]),
                                            ALU.mult).then_inc(rotated, 1)

            def silu(u):
                name, t = UNITS[u]
                e, half = STAGED.index(u), ["zA", "zB", "zC0", "zC1"].index(name) % 2
                dve.wait_ge(staged, e + 1)
                if name[1] == "C":
                    dve.wait_ge(turned, BATCH[1, t, 1] - FIRST_TURNED + 1)
                else:
                    dve.wait_ge(a_lo_done, 4 * 2 * T)
                nc.vector.scalar_tensor_tensor(out=act_src[:, t, half * NCOL:(half + 1) * NCOL],
                                               in0=stage2[:, e % 2, :], scalar=1.0, in1=stage[:, e % 2, :],
                                               op0=ALU.add, op1=ALU.mult).then_inc(silu_done, 1)

            def gate(layer, t, half):
                heads = slice(half * CH, (half + 1) * CH)
                dve.wait_ge(head_copied, HC * layer + CH * (half + 1))
                dve.wait_ge(silu_done, ZU.index(UNIT[[["zA", "zB"], ["zC0", "zC1"]][layer][half], t]) + 1)
                g = act_src[:, t, half * NCOL:(half + 1) * NCOL].rearrange("p (h d) -> p h d", h=CH)
                nc.vector.tensor_tensor(g, g, y[:, t, heads, 0:HD], ALU.mult).then_inc(gated, 1)

            def mask(s):
                if s == 0:
                    dve.wait_ge(masks_in, 48)
                mixer, h = STEPS[s]
                c = s if s < HC else s - HC
                m = masks[:, "ABC".index(mixer), :]
                need = mixer if mixer != "C" else f"C{h // CH}"
                dve.wait_ge(scores_done, s + 1)
                dve.wait_ge(qk_rstd, SCORES_NEED[need] + 1)
                if s == HC:
                    dve.wait_ge(const_done, 9)
                if s >= PROBS:
                    dve.wait_ge(probs_turned, s - PROBS + 1)
                first = BIG if mixer != "C" else neg_sinks[:, h:h + 1]
                for t, cols, mk in ((0, slice(0, P), m[:, P:2 * P]), (1, slice(P, 3 * P), m)):
                    last = nc.vector.tensor_tensor_reduce(out=probs[:, s % PROBS, cols], in0=sc[s % 2][:, cols], in1=mk,
                                                          scale=query_scale(mixer, h, t), scalar=first,
                                                          op0=ALU.add, op1=ALU.min, accum_out=neg_m[:, c, t:t + 1])
                last.then_inc(masked, 1)

            def count_probs(s):
                dve.wait_ge(probs_turned, s + 1)
                dve.wait_ge(masks_in, 48)
                if s >= 2:
                    dve.wait_ge(head_done, s - 1)
                nc.vector.tensor_tensor(probs_t[:, s % 2, :], tp[JOB["probs", s] % 2][:, 0:3 * P], count_t[:],
                                        ALU.mult).then_inc(probs_counted, 1)

            def copy_head(s):
                c = s if s < HC else s - HC
                o = ob[s % 2][:, 0:2 * VW].rearrange("p (t d) -> p t d", t=T)
                dve.wait_ge(head_done, s + 1)
                if s >= HC:
                    dve.wait_ge(gated, 4)
                    dve.wait_ge(sink_done, c + 1)
                    chain(nc.vector.scalar_tensor_tensor(out=inv_l[:, c, :], in0=sink_e[:, c, :], scalar=2.0,
                                                         in1=o[:, :, HD], op0=ALU.mult, op1=ALU.add))
                    chain(nc.vector.reciprocal(inv_l[:, c, :], inv_l[:, c, :]))
                else:
                    chain(nc.vector.reciprocal(inv_l[:, c, :], o[:, :, HD]))
                nc.vector.tensor_tensor(y[:, :, c, 0:HD], o[:, :, 0:HD],
                                        inv_l[:, c, :].rearrange("p (t o) -> p t o", o=1).to_broadcast([P, T, HD]),
                                        ALU.mult).then_inc(head_copied, 1)

            def add_residual(u, side=None):
                name, t = UNITS[u]
                c, width = int(name[1]) * NCOL, NCOL
                bank = acc[u % 2]
                if side is not None:
                    width, bank = NCOL // 2, acc[(u + side) % 2]
                    c += side * width
                at = c % NCOL
                dve.wait_ge(proj_done, u + 1 + (side or 0))
                if name[0] == "p":
                    dve.wait_ge(turned, BATCH[2, t, 1] - FIRST_TURNED + 1)
                    dve.wait_ge(sumsq_done, 8)
                nc.vector.tensor_tensor(x_sb[:, t, c:c + width], x_sb[:, t, c:c + width], bank[:, at:at + width],
                                        ALU.add).then_inc(out_added, 1)

            def read_units(n):
                for u in range(len(UNITS)):
                    if n == END[u] + 1:
                        if u in QK:
                            rotate(u)
                        elif u in ZU:
                            silu(u)
                        elif is_out(u):
                            add_residual(u)

            batch_lo(0)
            batch_lo(1)
            for p in SPLIT_AT[-1]:
                split_lo(p)
            for n in range(N_SLOTS):
                if n in DVE_SPLIT_FIRST:
                    for p in SPLIT_AT[n]:
                        split_lo(p)
                if n in DVE_UNIT_FIRST:
                    read_units(n)
                if n in STEP_AT:
                    mask(STEP_AT[n])
                if n in PROBS_AT and PROBS_AT[n] < HA:
                    count_probs(PROBS_AT[n])
                if n in VALUE_AT:
                    copy_head(VALUE_AT[n])
                for g in GATE_AT.get(n, []):
                    if not gate_after_silu(g):
                        gate(*g)
                for b in BATCH_AT.get(n, []):
                    if b >= 2:
                        batch_lo(b)
                if n not in DVE_UNIT_FIRST:
                    read_units(n)
                for g in GATE_AT.get(n, []):
                    if gate_after_silu(g):
                        gate(*g)
                if n not in DVE_SPLIT_FIRST:
                    for p in SPLIT_AT[n]:
                        split_lo(p)
            for side in range(2):
                add_residual(LAST, side)


def packed_weights(even_in, even_out, odd_in, odd_out):
    heads = np.array([p // 2 + 8 * (p % 2) for p in range(HC)])
    cols = (heads[:, None] * HD + np.arange(HD)[None, :]).reshape(-1)
    width = HC * HD
    cut = {}
    for i, n in enumerate(("qA", "kA", "vA", "zA", "qB", "kB", "vB", "zB")):
        cut[n] = even_in[:, i * NCOL:(i + 1) * NCOL]
    q, kv, z = odd_in[:, 0:width][:, cols], odd_in[:, width:width + 256], odd_in[:, width + 256:][:, cols]
    out = odd_out[cols, :]
    cut["kvC"] = kv
    for i in range(2):
        half = slice(i * NCOL, (i + 1) * NCOL)
        cut[f"o{i}"], cut[f"qC{i}"], cut[f"zC{i}"], cut[f"p{i}"] = even_out[:, half], q[:, half], z[:, half], out[:, half]
    rows = []
    for name, w in CHUNKS:
        c = cut[name].reshape(K, P, w).transpose(1, 0, 2).reshape(P, -1, PER_DMA * PIECE)
        rows.append(c.transpose(1, 0, 2))
    return np.ascontiguousarray(np.concatenate(rows)), heads


def tables():
    inv = np.float32(ROPE_THETA) ** (-np.arange(0, HD, 2, dtype=np.float32) / np.float32(HD))
    ang = np.arange(S, dtype=np.float32)[:, None] * inv[None, :].astype(np.float32)
    cos, sin = np.cos(ang), np.sin(ang)
    i = np.arange(P)[:, None]
    dist = np.concatenate([P + i - np.arange(P)[None, :], i - np.arange(P)[None, :]], axis=1)
    count = sum(((dist >= 0) & (dist <= w) & (dist % d == 0)).astype(np.float32)
                for w, d in ((128, 1), (512, 4), (2048, 16)))
    keep = [count > 0, dist >= 0, (dist >= 0) & (dist < WINDOW)]
    prev, own = count[:, :P].T, count[:, P:].T
    m = np.concatenate([np.where(k, 0.0, NEG) for k in keep] + [own, prev, own], axis=1).astype(np.float32)
    return (np.concatenate([cos, cos], axis=1).astype(np.float32),
            np.concatenate([-sin, sin], axis=1).astype(np.float32), np.ascontiguousarray(m))


def kernel(**inputs):
    import concourse.bacc as bacc
    from concourse.bass_utils import run_bass_kernel_spmd as run

    a = {k: np.asarray(v) for k, v in inputs.items()}
    w, heads = packed_weights(a["w_in_even"][0], a["w_out_even"][0], a["w_in_odd"][0], a["w_out_odd"][0])
    g = [a[k][0] for k in ("qnorm_a", "knorm_a", "qnorm_b", "knorm_b", "qnorm_c", "knorm_c")]
    swapped = [np.concatenate([v[HD // 2:], v[:HD // 2]]) for v in g]
    cos, sin, masks = tables()
    arrays = {
        "x": a["x"][0],
        "xt": a["x"][0].reshape(T, P, 2, K // 2, P).transpose(0, 2, 4, 3, 1).reshape(2 * T, P, NCOL),
        "w": w,
        "gains": np.concatenate([a[k][0].reshape(K, P).T for k in ("norm_even", "norm_odd")], axis=1),
        "heads": np.concatenate(g + swapped)[None, :],
        "cos": cos,
        "sin": sin,
        "masks": masks,
        "sinks": a["sinks_c"][0][heads][None, :],
    }
    arrays = {k: np.ascontiguousarray(v) for k, v in arrays.items()}
    nc = bacc.Bacc("TRN2", target_bir_lowering=False, num_devices=1)
    args = [nc.dram_tensor(f"in_{k}", v.shape, mybir.dt.from_np(v.dtype), kind="ExternalInput").ap()
            for k, v in arrays.items()]
    out = nc.dram_tensor("out", (S, D), F32, kind="ExternalOutput").ap()
    hybrid_trunk(nc, *args, out)
    got = run(nc, [{f"in_{k}": v for k, v in arrays.items()}], core_ids=[0])
    return got.results[0]["out"].reshape(1, S, D)
```
